# Optimizing a Trainium2 kernel written in Bass

```python
import jax, jax.numpy as jnp
from jax import lax
import numpy as np

D_MODEL = 1024
BATCH = 1
SEQ = 1024
DEPTH = 1
DEC_BATCH = 8
DEC_SEQ = 8
PAST_LEN = 256
PAGE_SIZE = 128

CONV_WIDTH = D_MODEL // 2
SB_HEADS = 8
SB_HEAD_DIM = 64
SB_WIDTH = SB_HEADS * SB_HEAD_DIM
KSIZE = 3
D_FF = 2816
PLE_DIM = 256
Q_BLOCK = 128
EPS = 1e-6
SB_BIAS_INIT = -6.0
IN_SIZES = [CONV_WIDTH] * 3 + [SB_WIDTH] * 3 + [D_MODEL] * 2
N_IN = sum(IN_SIZES)
IN_SPLITS = np.cumsum(IN_SIZES)[:-1].tolist()

kernel_name = "gated_shortconv_stickbreaking_convffn_decode_step"

def rms_norm(x, g):
    xf = x.astype(jnp.float32)
    y = xf * lax.rsqrt(jnp.mean(xf * xf, axis=-1, keepdims=True) + EPS)
    return (y * g.astype(jnp.float32)).astype(x.dtype)

def causal_dwconv(u, prev, w, b=None):
    t = u.shape[1]
    full = jnp.concatenate([prev.astype(u.dtype), u], axis=1)
    y = w[0] * full[:, 0:t]
    for j in range(1, KSIZE):
        y = y + w[j] * full[:, j:j + t]
    if b is not None:
        y = y + b
    return y, full[:, t:]

def sb_block(q, k, v, bias, q_pos, k_pos):
    z = jnp.einsum('bqhd,bkhd->bhqk', q.astype(jnp.float32), k.astype(jnp.float32)) * (SB_HEAD_DIM ** -0.5)
    z = z + bias.astype(jnp.float32)[None, :, None, None]
    mask = k_pos[None, :] < q_pos[:, None]
    log_beta = jax.nn.log_sigmoid(z)
    log_keep = jnp.where(mask, jax.nn.log_sigmoid(-z), 0.0)
    later = lax.cumsum(log_keep, axis=3, reverse=True) - log_keep
    a = jnp.where(mask, jnp.exp(log_beta + later), 0.0)
    return jnp.einsum('bhqk,bkhd->bqhd', a, v.astype(jnp.float32))

def stick_breaking(q, k, v, bias):
    t = q.shape[1]
    off = k.shape[1] - t
    outs = []
    for s in range(0, t, Q_BLOCK):
        e = min(s + Q_BLOCK, t)
        kend = off + e
        q_pos = off + jnp.arange(s, e)
        k_pos = jnp.arange(kend)
        outs.append(sb_block(q[:, s:e], k[:, :kend], v[:, :kend], bias, q_pos, k_pos))
    return jnp.concatenate(outs, axis=1)

def trunk_layer(x, p, k_past, v_past, conv_prev, ffn_prev,
                g_pre_mix, w_in, w_conv_a, w_a, w_b, sb_bias, w_o, g_post_mix,
                g_pre_ffn, w_up, w_conv_f, b_conv_f, w_down, g_post_ffn,
                w_ple, g_ple_gate, w_ple_gate, g_post_ple):
    bsz, t, _ = x.shape
    h = rms_norm(x, g_pre_mix)
    cb, cc, ch, q, k, v, ga, gb = jnp.split(h @ w_in, IN_SPLITS, axis=-1)
    conv_u, conv_state = causal_dwconv(cc * ch, conv_prev, w_conv_a)
    y_a = (cb * conv_u) @ w_a
    q = q.reshape(bsz, t, SB_HEADS, SB_HEAD_DIM)
    k = k.reshape(bsz, t, SB_HEADS, SB_HEAD_DIM)
    v = v.reshape(bsz, t, SB_HEADS, SB_HEAD_DIM)
    k_all = jnp.concatenate([k_past.astype(k.dtype), k], axis=1)
    v_all = jnp.concatenate([v_past.astype(v.dtype), v], axis=1)
    o = stick_breaking(q, k_all, v_all, sb_bias).astype(x.dtype).reshape(bsz, t, SB_WIDTH)
    y_b = o @ w_b
    merged = jax.nn.sigmoid(ga) * y_a + jax.nn.sigmoid(gb) * y_b
    x = x + rms_norm(merged @ w_o, g_post_mix)
    up, ffn_state = causal_dwconv(rms_norm(x, g_pre_ffn) @ w_up, ffn_prev, w_conv_f, b_conv_f)
    gate, val = jnp.split(up, 2, axis=-1)
    x = x + rms_norm((jax.nn.gelu(gate) * val) @ w_down, g_post_ffn)
    e = (p @ w_ple) * jax.nn.sigmoid(rms_norm(x, g_ple_gate) @ w_ple_gate)
    x = x + rms_norm(e, g_post_ple)
    return x, k, v, conv_state, ffn_state

def setup_inputs(seed: int = 0) -> dict:
    key = jax.random.key(seed)
    ks = iter(jax.random.split(key, 40))
    f32 = jnp.float32
    n_pages = PAST_LEN // PAGE_SIZE
    n_used = DEC_BATCH * n_pages
    n_pool = n_used + n_used // 4

    def nrm(shape, scale=1.0):
        return jax.random.normal(next(ks), shape, f32) * scale

    def gain(shape):
        return 1.0 + 0.05 * jax.random.normal(next(ks), shape, f32)

    x_prompt = nrm((BATCH, SEQ, D_MODEL))
    x_sample = nrm((DEC_BATCH, DEC_SEQ, D_MODEL))
    cache_k = nrm((DEPTH, n_pool, PAGE_SIZE, SB_HEADS, SB_HEAD_DIM))
    cache_v = nrm((DEPTH, n_pool, PAGE_SIZE, SB_HEADS, SB_HEAD_DIM))
    state_conv = nrm((DEPTH, DEC_BATCH, KSIZE - 1, CONV_WIDTH))
    state_ffn_conv = nrm((DEPTH, DEC_BATCH, KSIZE - 1, 2 * D_FF))
    page_table = jax.random.permutation(next(ks), n_pool)[:n_used].reshape(DEC_BATCH, n_pages).astype(jnp.int32)
    p_prompt = nrm((DEPTH, BATCH, SEQ, PLE_DIM))
    p_sample = nrm((DEPTH, DEC_BATCH, DEC_SEQ, PLE_DIM))
    return {
        "x_prompt": x_prompt, "x_sample": x_sample,
        "cache_k": cache_k, "cache_v": cache_v,
        "state_conv": state_conv, "state_ffn_conv": state_ffn_conv,
        "page_table": page_table, "p_prompt": p_prompt, "p_sample": p_sample,
        "g_pre_mix": gain((DEPTH, D_MODEL)),
        "w_in": nrm((DEPTH, D_MODEL, N_IN), D_MODEL ** -0.5),
        "w_conv_a": nrm((DEPTH, KSIZE, CONV_WIDTH), KSIZE ** -0.5),
        "w_a": nrm((DEPTH, CONV_WIDTH, D_MODEL), CONV_WIDTH ** -0.5),
        "w_b": nrm((DEPTH, SB_WIDTH, D_MODEL), SB_WIDTH ** -0.5),
        "sb_bias": SB_BIAS_INIT + nrm((DEPTH, SB_HEADS), 0.1),
        "w_o": nrm((DEPTH, D_MODEL, D_MODEL), D_MODEL ** -0.5),
        "g_post_mix": gain((DEPTH, D_MODEL)),
        "g_pre_ffn": gain((DEPTH, D_MODEL)),
        "w_up": nrm((DEPTH, D_MODEL, 2 * D_FF), D_MODEL ** -0.5),
        "w_conv_f": nrm((DEPTH, KSIZE, 2 * D_FF), KSIZE ** -0.5),
        "b_conv_f": nrm((DEPTH, 2 * D_FF), 0.01),
        "w_down": nrm((DEPTH, D_FF, D_MODEL), D_FF ** -0.5),
        "g_post_ffn": gain((DEPTH, D_MODEL)),
        "w_ple": nrm((DEPTH, PLE_DIM, D_MODEL), PLE_DIM ** -0.5),
        "g_ple_gate": gain((DEPTH, D_MODEL)),
        "w_ple_gate": nrm((DEPTH, D_MODEL, D_MODEL), D_MODEL ** -0.5),
        "g_post_ple": gain((DEPTH, D_MODEL)),
    }

def reference(x_prompt, x_sample, cache_k, cache_v, state_conv, state_ffn_conv, page_table,
              p_prompt, p_sample, g_pre_mix, w_in, w_conv_a, w_a, w_b, sb_bias, w_o, g_post_mix,
              g_pre_ffn, w_up, w_conv_f, b_conv_f, w_down, g_post_ffn,
              w_ple, g_ple_gate, w_ple_gate, g_post_ple):
    n_pages = PAST_LEN // PAGE_SIZE
    nb_p = x_prompt.shape[0]
    nb_s = x_sample.shape[0]
    xp, xs = x_prompt, x_sample
    kp_l, vp_l, cp_l, fp_l = [], [], [], []
    ks_l, vs_l, cs_l, fs_l = [], [], [], []
    for i in range(DEPTH):
        lw = (g_pre_mix[i], w_in[i], w_conv_a[i], w_a[i], w_b[i], sb_bias[i], w_o[i], g_post_mix[i],
              g_pre_ffn[i], w_up[i], w_conv_f[i], b_conv_f[i], w_down[i], g_post_ffn[i],
              w_ple[i], g_ple_gate[i], w_ple_gate[i], g_post_ple[i])
        empty_kv = jnp.zeros((nb_p, 0, SB_HEADS, SB_HEAD_DIM), xp.dtype)
        xp, kp, vp, cp, fp = trunk_layer(
            xp, p_prompt[i], empty_kv, empty_kv,
            jnp.zeros((nb_p, KSIZE - 1, CONV_WIDTH), xp.dtype),
            jnp.zeros((nb_p, KSIZE - 1, 2 * D_FF), xp.dtype), *lw)
        k_past = cache_k[i][page_table].reshape(nb_s, n_pages * PAGE_SIZE, SB_HEADS, SB_HEAD_DIM)
        v_past = cache_v[i][page_table].reshape(nb_s, n_pages * PAGE_SIZE, SB_HEADS, SB_HEAD_DIM)
        xs, ksm, vsm, csm, fsm = trunk_layer(
            xs, p_sample[i], k_past, v_past, state_conv[i], state_ffn_conv[i], *lw)
        kp_l.append(kp); vp_l.append(vp); cp_l.append(cp); fp_l.append(fp)
        ks_l.append(ksm); vs_l.append(vsm); cs_l.append(csm); fs_l.append(fsm)
    return (xp, xs,
            jnp.stack(kp_l), jnp.stack(vp_l), jnp.stack(cp_l), jnp.stack(fp_l),
            jnp.stack(ks_l), jnp.stack(vs_l), jnp.stack(cs_l), jnp.stack(fs_l))


_drawn_inputs = setup_inputs


def setup_inputs(seed=0):
    import zlib

    import numpy as np

    out = dict(_drawn_inputs(seed))
    spreads = {}
    factors = {'sb_bias': 8.0, 'b_conv_f': 7.739, 'g_ple_gate': 5.719}
    for name, (base, spread) in spreads.items():
        noise = np.random.default_rng([zlib.crc32(name.encode()), seed]).standard_normal(out[name].shape)
        drawn = base * np.exp(spread * noise) if base else spread * noise
        out[name] = __import__('jax').numpy.asarray(drawn.astype(out[name].dtype))
    for name, factor in factors.items():
        out[name] = (out[name] * factor).astype(out[name].dtype)
    return out
```

```python
from contextlib import ExitStack, contextmanager

import concourse.bass as bass
from concourse import mybir

F32 = mybir.dt.float32
F32R = mybir.dt.float32r
I32 = mybir.dt.int32
ALU = mybir.AluOpType
ACT = mybir.ActivationFunctionType
ds = bass.ds

P = 128
D = 1024
KD = D // P
SEQ = 1024
NB, NT = 8, 8
NS = NB * NT
TOK = SEQ + NS
GROUPS = [(0, 384), (384, 384), (768, 320)]
NG = 3
BLK = SEQ // P
CW = 512
NC4 = CW // P
FF = 2816
NFF = FF // P
PLE = 256
PAGES = 2
EPS = 1e-6
SCALE = 64 ** -0.5
FAR = -1.0e30 / SCALE
UW = SEQ + 2 + NB * (NT + 2)
US = SEQ + 2
GAINS = ["g_pre_mix", "g_post_mix", "g_pre_ffn", "g_post_ffn", "g_ple_gate", "g_post_ple"]

STEPS = [(h, qh, kb) for h in range(2) for qh in range(2) for kb in range(4 * qh + 3, -1, -1)]
NPS = len(STEPS)
NSTEP = NPS + 1
SAMPLE = NPS
SLOTS = NSTEP + 3
IN_FILL = 21
PIECES = IN_FILL * KD // SLOTS
assert PIECES * SLOTS == IN_FILL * KD
AHEAD = 2
FILL_AT = {(KD * i + KD - 1) // PIECES: i for i in range(IN_FILL)}
M_ITER = 18
PM_ITER = 13


def step_shape(s):
    if s == SAMPLE:
        return 0, 384, True, True, True
    h, qh, kb = STEPS[s]
    q0 = max(kb * P, qh * 512)
    return q0 - qh * 512, qh * 512 + 512 - q0, kb >= 4 * qh, kb == 4 * qh + 3, kb == 0


COMPS = [s for s in range(NSTEP) if not step_shape(s)[4]]


def job_ends():
    n, ends = 27, []
    for units in ([3] * 40 + [6] * 8 + [3] * 8 + [(30, 3)] + [3] * 3 + [3, 3, 12, 12, 3, 3] * 10 + [12] * 2
                  + [(9, 12), 12] + [(3, 3)] + [3] * 7):
        gap, k = units if isinstance(units, tuple) else (0, units)
        n += gap + k
        ends.append(n)
    return ends


ENDS = job_ends()


class Count:

    def __init__(self):
        self.base, self.turn = 0, None

    def at(self, d=0):
        v = self.base + d
        return v if self.turn is None else v + self.turn

    def step(self, k=1):
        self.base += k
        return self.at()


@contextmanager
def loop(eng, n, adds):
    with eng.Fori(0, n) as it:
        before = {c: c.base for c in adds}
        for c, per in adds.items():
            c.turn = it * per
        yield it
        for c, per in adds.items():
            assert c.base - before[c] == per, (list(adds.values()), [x.base - before[x] for x in adds])
            c.turn = None
    for c, per in adds.items():
        c.base = before[c] + n * per


def build(nc, inp, out, gate_spill):
    with ExitStack() as ctx:
        def sem(name):
            return ctx.enter_context(nc.semaphore(name))

        BASE = 16512
        TOP = 229368

        def at(name, shape, offset, dt=F32):
            size = 4
            for x in shape[1:]:
                size *= x
            assert BASE + offset + size <= TOP, (name, offset + size)
            return nc.alloc_sbuf_tensor_at(name, shape, dt, offset=BASE + offset)

        class Region:
            def __init__(self, start, end):
                self.p, self.end = start, end

            def take(self, name, shape, dt=F32):
                size = 4
                for x in shape[1:]:
                    size *= x
                t = at(name, shape, self.p, dt)
                self.p += (size + 31) // 32 * 32
                assert self.p <= self.end, (name, self.p, self.end)
                return t

        ACTS = 8 * TOK * 4
        R1, R2, R3 = 0, 2 * ACTS, 4 * ACTS
        RTOP = TOP - BASE
        xh = at("xh", [P, KD, TOK], R1, F32R)
        xl = at("xl", [P, KD, TOK], R1 + ACTS, F32R)
        a = Region(R1, R2)
        ch, cl, oh, ol = (a.take(n, [P, NC4, TOK], F32R) for n in ("ch", "cl", "oh", "ol"))
        y = at("y", [P, KD, TOK], R1)
        xn2 = at("xn2", [P, BLK, D], R1 + ACTS)
        a = Region(R1 + ACTS, R2)
        fh, fl = a.take("fh", [P, 2, TOK], F32R), a.take("fl", [P, 2, TOK], F32R)
        pn = at("pn", [P, BLK + 1, PLE], R2 - 9 * PLE * 4)
        ple = at("ple", [P, KD, TOK], R1 + ACTS)
        on = at("on", [P, 2, 3, D], R1 + ACTS)
        xn = at("xn", [P, BLK + 1, D], R2)
        cout = at("cout", [P, NC4, TOK], R2)
        oT = at("oT", [P, NC4, TOK], R2 + NC4 * TOK * 4)
        bh = at("bh", [P, KD, TOK], R2, F32R)
        bl = at("bl", [P, KD, TOK], R2 + ACTS, F32R)
        a = Region(R3, RTOP)
        raw = [a.take(f"raw{i}", [P, 1024]) for i in range(2)]
        wh = [a.take(f"wh{i}", [P, 1024], F32R) for i in range(2)]
        wl = [a.take(f"wl{i}", [P, 1024], F32R) for i in range(2)]
        rs = a.take("rs", [P, TOK])
        ident = a.take("ident", [P, P])
        ones = a.take("ones", [P, P])
        tri = a.take("tri", [P, P], F32R)
        comp = a.take("comp", [P, P], F32R)
        full = a.take("full", [P, P], F32R)
        far = a.take("far", [P, P])
        fars = a.take("fars", [P, 384])
        bfars = a.take("bfars", [P, 384])
        gains = a.take("gains", [P, 6 * KD])
        bias = a.take("bias", [P, 8])
        bias2 = a.take("bias2", [P, 8])
        eps = a.take("eps", [P, 8])
        qbd = a.take("qbd", [P, NB, 2, NT])
        R3T = a.p
        a = Region(R3T, RTOP)
        ss = a.take("ss", [P, TOK])
        sq = [a.take(f"sq{i}", [P, 384]) for i in range(2)]
        tmp = [a.take(f"tmp{i}", [P, 384]) for i in range(2)] + [at("tmp2", [P, 384], (RTOP - 384 * 4) // 32 * 32)]
        NORM = a.p
        ms, rt, t1 = (a.take(n, [P, TOK]) for n in ("ms", "rt", "t1"))
        xn2s = a.take("xn2s", [NS, D])
        trif, compf = a.take("trif", [P, P]), a.take("compf", [P, P])
        gnat = a.take("gnat", [6 * KD, P])
        brow = a.take("brow", [1, 8])
        a = Region(R2 + ACTS, R3)
        qT, kT, vT = (a.take(n, [P, TOK]) for n in ("qT", "kT", "vT"))
        pk = at("pk", [P, 2, 4, P], a.p - TOK * 4)
        vn = a.take("vn", [P, BLK + 1, P])
        pkT = a.take("pkT", [P, PAGES * NB * P])
        a2 = Region(R3T, RTOP)
        pv = a2.take("pv", [P, PAGES * NB, P])
        uc = a2.take("uc", [P, UW])
        tm1 = a.take("tm1", [P, 384])
        stg = [a2.take(f"stg{i}", [P, 384]) for i in range(NG)]
        z = [a2.take(f"z{i}", [P, 512]) for i in range(3)]
        tt = [a2.take(f"tt{i}", [P, 512]) for i in range(2)]
        lh = [a2.take(f"lh{i}", [P, 512], F32R) for i in range(2)]
        ll = [a2.take(f"ll{i}", [P, 512], F32R) for i in range(2)]
        aa = [a.take(f"aa{i}", [P, 512]) for i in range(2)]
        cwr = a.take("cwr", [2 * NB + 3, P])
        so = a.take("so", [P, 18])
        sot = a2.take("sot", [2 * NB, 2, P])
        cwt = a2.take("cwt", [P, 19])
        pgt = a2.take("pgt", [1, NB * PAGES], I32)
        a = Region(R3T, RTOP)
        gat = [a.take(f"gat{i}", [P, TOK]) for i in range(4)]
        ma = [a.take(f"ma{i}", [P, 384]) for i in range(3)]
        mb = [a.take(f"mb{i}", [P, 384]) for i in range(3)]
        a = Region(NORM, RTOP)
        ug, uv = a.take("ug", [P, UW]), a.take("uv", [P, UW])
        cg = a.take("cg", [P, TOK])
        a = Region(a.p, RTOP)
        cv = a.take("cv", [P, TOK])
        fr = a.take("fr", [20, 2, P])
        fw = [a.take(f"fw{i}", [P, 2, 20]) for i in range(2)]
        fso = a.take("fso", [P, 2, 18])
        fsot = a.take("fsot", [18, 2, P])
        a = Region(NORM + 2 * TOK * 4, RTOP)
        pl, ph = a.take("pl", [P, 2, TOK], F32R), a.take("ph", [P, 2, TOK], F32R)

        def f(t):
            return t.bitcast(F32)

        banks = [nc.alloc_psum_tensor(f"bank{i}", [P, 512], F32) for i in range(8)]
        ub = banks[0:3]
        sb_ = banks[3:5]
        pb_ = banks[5]
        mb_ = banks[6:8]

        x_in = [sem(f"x_in{g}") for g in range(NG)]
        const_in = sem("const_in")
        page_in = sem("page_in")
        raw_in = [sem("raw_in0"), sem("raw_in1")]
        pk_in = [sem("pk_in0"), sem("pk_in1")]
        pv_in = sem("pv_in")
        cwr_in = sem("cwr_in")
        gat_in = [sem("gat_in0"), sem("gat_in1")]
        x2_in = sem("x2_in")
        p_in = sem("p_in")
        stg_out = [sem(f"stg_out{g}") for g in range(NG)]
        vn_out = sem("vn_out")
        so_out = sem("so_out")
        y_out = [sem("y_out0"), sem("y_out1")]
        g_const = sem("g_const")
        g_fold = sem("g_fold")
        g_ss = sem("g_ss")
        g_self = sem("g_self")
        g_xl = sem("g_xl")
        g_acc0 = sem("g_acc0")
        a_hi = sem("a_hi")
        a_sq = sem("a_sq")
        a_m = sem("a_m")
        a_abs, a_exp, a_ln, a_lhi, a_a = (sem(n) for n in ("a_abs", "a_exp", "a_ln", "a_lhi", "a_a"))
        a_rt = sem("a_rt")
        a_self = sem("a_self")
        a_xhi = sem("a_xhi")
        a_sig = sem("a_sig")
        a_gelu = sem("a_gelu")
        d_const = sem("d_const")
        d_lo = sem("d_lo")
        d_unit = sem("d_unit")
        d_r = sem("d_r")
        d_self = sem("d_self")
        d_qbd = sem("d_qbd")
        d_z, d_sp, d_llo, d_sub = (sem(n) for n in ("d_z", "d_sp", "d_llo", "d_sub"))
        d_so = sem("d_so")
        d_t = sem("d_t")
        d_x = sem("d_x")
        d_xlo = sem("d_xlo")
        d_mrg = sem("d_mrg")
        d_cg = sem("d_cg")
        d_act = sem("d_act")
        d_e = sem("d_e")
        sp_held, pe_held = sem("sp_held"), sem("pe_held")
        p_const = sem("p_const")
        p_unit = sem("p_unit")
        p_m = sem("p_m")
        p_s, p_tri, p_comp, p_av = (sem(n) for n in ("p_s", "p_tri", "p_comp", "p_av"))

        xp = inp["x_prompt"].rearrange("n (b p) d -> p (n b) d", p=P)
        xsm = inp["x_sample"].rearrange("b t d -> (b t) d")
        ck = inp["cache_k"].rearrange("l n p h d -> (l n) p (h d)")
        cvv = inp["cache_v"].rearrange("l n p h d -> (l n) p (h d)")
        NPOOL = ck.shape[0]
        w_in = inp["w_in"].rearrange("l (k p) n -> p (l k) n", p=P)
        w_a = inp["w_a"].rearrange("l (k p) n -> p (l k) n", p=P)
        w_b = inp["w_b"].rearrange("l (k p) n -> p (l k) n", p=P)
        w_o = inp["w_o"].rearrange("l (k p) n -> p (l k) n", p=P)
        w_up = inp["w_up"].rearrange("l (k p) n -> p (l k) n", p=P)
        w_down = inp["w_down"].rearrange("l (k p) n -> p (l k) n", p=P)
        w_ple = inp["w_ple"].rearrange("l (k p) n -> p (l k) n", p=P)
        w_gate = inp["w_ple_gate"].rearrange("l (k p) n -> p (l k) n", p=P)
        pp = inp["p_prompt"].rearrange("l n (b p) d -> p (l n b) d", p=P)
        psm = inp["p_sample"].rearrange("l b t d -> (l b t) d")
        st_c = inp["state_conv"].rearrange("l b t c -> (l b t) c")
        st_f = inp["state_ffn_conv"].rearrange("l b t c -> (l b t) c")
        wc = inp["w_conv_a"].rearrange("l t c -> (l t) c")
        wf = inp["w_conv_f"].rearrange("l t c -> (l t) c")
        yp_o = out["y_prompt"].rearrange("n (b p) d -> p (n b) d", p=P)
        ys_o = out["y_sample"].rearrange("b t d -> (b t) d")
        kp_o, vp_o = (out[n].rearrange("l n (b p) h d -> p (l n b) (h d)", p=P) for n in ("k_prompt", "v_prompt"))
        ks_o, vs_o = (out[n].rearrange("l b t h d -> (l b t) (h d)") for n in ("k_sample", "v_sample"))
        cp_o = out["conv_prompt"].rearrange("l n t c -> (l n t) c")
        cs_o = out["conv_sample"].rearrange("l b t c -> (l b t) c")
        fp_o = out["ffn_conv_prompt"].rearrange("l n t c -> (l n t) c")
        fs_o = out["ffn_conv_sample"].rearrange("l b t c -> (l b t) c")

        IN_COLS = [(3 * CW, P), (4 * CW, P), (5 * CW, P), (CW, P), (2 * CW, P), (0, P),
                   (6 * CW, 2 * P), (6 * CW + P, 2 * P), (6 * CW + D, 2 * P), (6 * CW + D + P, 2 * P)]
        NIN = len(IN_COLS)
        NJOBS = NIN * NC4 + 8 + 8 + 4 + 60 + 2 + 2 + 8

        def block_rows(b):
            return P if b < BLK else NS

        def group_blocks(g):
            return range(3 * g, 3 * g + 3)

        def part(t, g):
            o, w = GROUPS[g]
            return t[..., o:o + w]

        def padded(t, g):
            o, w = GROUPS[g]
            if g < 2:
                return [(t[:, 2 + o:2 + o + w], slice(0, w))]
            return [(t[:, 2 + o:2 + SEQ], slice(0, SEQ - o)),
                    (t[:, US:UW].rearrange("p (b t) -> p b t", t=NT + 2)[:, :, 2:], slice(SEQ - o, w))]

        def like(ap, ref):
            return ap.rearrange("p (b t) -> p b t", t=NT) if len(ref.shape) == 3 else ap

        block = ctx.enter_context(nc.Block())

        @block.sync
        def _(sp):
            def hold(sem_, value):
                sp.wait_ge(sem_, value)
                sp.sem_inc(sp_held, 1)

            job = Count()

            def load(parts):
                if job.base >= 2:
                    hold(d_lo, job.at(-1))
                s = job.base % 2
                for dst, src in parts(raw[s]):
                    sp.dma_start(dst, src).then_inc(raw_in[s], 16)
                job.step()

            def tall(w, col):
                def parts(r):
                    r = r[:, :].rearrange("p (k n) -> p k n", n=P)
                    return [(r[:, 4 * i:4 * i + 4, :], w[:, 4 * i:4 * i + 4, ds(col, P)]) for i in range(2)]
                return parts

            def wide(w, k, col):
                def parts(r):
                    r = r[:, :].rearrange("p (k n) -> p k n", n=512)
                    return [(r[:, i:i + 1, :], w[:, ds(k + i, 1), col:col + 512]) for i in range(2)]
                return parts

            def in_job(c, n):
                start, stride = IN_COLS[n]
                return tall(w_in, c * stride + start)

            for i, n in enumerate(GAINS):
                sp.dma_start(gnat[i * KD:(i + 1) * KD, :], inp[n].rearrange("l (k p) -> (l k) p", p=P)).then_inc(const_in, 16)
            sp.dma_start(brow[:, :], inp["sb_bias"]).then_inc(const_in, 16)
            for g in range(NG):
                bs = [b for b in group_blocks(g) if b < BLK]
                sp.dma_start(xn[:, bs[0]:bs[-1] + 1, :], xp[:, bs[0]:bs[-1] + 1, :]).then_inc(x_in[g], 16)
                if g == NG - 1:
                    sp.dma_start(xn[0:NS, BLK, :], xsm).then_inc(x_in[g], 16)
                if g == 0:
                    load(in_job(0, 0))
                    load(in_job(0, 1))
            hold(d_r, NG)
            sp.dma_start(pgt[:, :], inp["page_table"].rearrange("b g -> (b g)").rearrange("(o n) -> o n", o=1)).then_inc(page_in, 16)
            hold(page_in, 16)

            miscn, avn = Count(), Count()
            miscn.base = 2

            def rows_in(c):
                sp.dma_start(cwr[0:2 * NB, :], st_c[:, ds(c * P, P)]).then_inc(cwr_in, 16)
                sp.dma_start(cwr[2 * NB:2 * NB + 3, :], wc[:, ds(c * P, P)]).then_inc(cwr_in, 16)

            def cached(c, q, dst, src, done):
                for i in range(4):
                    e = 4 * q + i
                    pg, b = 1 - e // NB, e % NB
                    page = sp.value_load(pgt[0:1, b * PAGES + pg:b * PAGES + pg + 1], min_val=0, max_val=NPOOL - 1)
                    sp.dma_start(dst(q, i), src[ds(page, 1), :, ds(c * P, P)].rearrange("o p d -> p (o d)")).then_inc(done, 16)

            def keys(c, q):
                cached(c, q, lambda q, i: pk[:, q % 2, i, :], ck, pk_in[q % 2])

            def values(c, q):
                cached(c, q, lambda q, i: pv[:, 4 * q + i, :], cvv, pv_in)

            def gate_out(c, n, back=0):
                half, sub = (n - 6) // 2, (n - 6) % 2
                for g in range(NG):
                    o, w = GROUPS[g]
                    hold(d_unit, unitn.at(3 * n + g + 1 - back))
                    sp.dma_start(gate_spill[ds(half * KD + sub + 2 * c, 1), :, o:o + w].rearrange("o p t -> p (o t)"),
                                 stg[g][:, 0:w]).then_inc(stg_out[g], 16)

            unitn = Count()
            unitn.base = 27

            def pair(c, last):
                load(in_job(c, 2))
                hold(p_m, miscn.at(2))
                keys(c, 2)
                load(in_job(c, 3))
                hold(p_m, miscn.at(3))
                keys(c, 3)
                for n in range(4, NIN):
                    load(in_job(c, n))
                    if n >= 8:
                        gate_out(c, n - 2)
                    if 4 <= n < 8:
                        if n == 4:
                            hold(p_av, avn.at())
                        values(c, n - 4)
                    if n == 7 and not last:
                        hold(p_m, miscn.at(11))
                        rows_in(c + 1)
                        keys(c + 1, 0)
                        keys(c + 1, 1)
                if not last:
                    load(in_job(c + 1, 0))
                    gate_out(c, NIN - 2)
                    load(in_job(c + 1, 1))
                    gate_out(c, NIN - 1)
                miscn.step(PM_ITER)
                avn.step(NSTEP)
                unitn.step(3 * NIN)

            rows_in(0)
            keys(0, 0)
            keys(0, 1)
            with loop(sp, NC4 - 1, {job: NIN, miscn: PM_ITER, avn: NSTEP, unitn: 3 * NIN}) as c:
                pair(c, False)
            pair(NC4 - 1, True)

            def ab_job(m):
                def parts(r):
                    r = r[:, :].rearrange("p (k n) -> p k n", n=P)
                    return [(r[:, 0:4, :], w_a[:, :, ds(m * P, P)]), (r[:, 4:8, :], w_b[:, :, ds(m * P, P)])]
                return parts

            load(ab_job(0))
            gate_out(NC4 - 1, NIN - 2, 3 * NIN)
            load(ab_job(1))
            gate_out(NC4 - 1, NIN - 1, 3 * NIN)
            per_g = [NC4 * 5, NC4 * 5, NC4 * 6]
            for g in range(NG):
                hold(stg_out[g], 16 * per_g[g])
            hold(d_unit, unitn.at())
            hold(vn_out, 16 * NC4 * 4)
            hold(so_out, 16 * NC4 * 2)
            hold(a_m, 2 + NC4 * M_ITER)

            mrg = Count()

            def gates(m, s):
                for h in range(2):
                    sp.dma_start(gat[2 * s + h][:, :], gate_spill[ds(h * KD + m, 1), :, :].rearrange("o p t -> p (o t)")).then_inc(gat_in[s], 16)

            gates(0, 0)
            gates(1, 1)
            with loop(sp, 3, {job: 2, mrg: 2 * NG}) as t:
                for s in range(2):
                    load(ab_job(t * 2 + 2 + s))
                    mrg.step(NG)
                    hold(d_mrg, mrg.at())
                    gates(t * 2 + 2 + s, s)
            load(tall(w_o, 0))
            load(tall(w_o, P))
            hold(p_unit, ENDS[47])
            hold(d_mrg, 8 * NG)
            sp.dma_start(xn2[:, :, :], xp).then_inc(x2_in, 16)
            sp.dma_start(xn2s[:, :], xsm).then_inc(x2_in, 16)
            with loop(sp, 3, {job: 2}) as t:
                for s in range(2):
                    load(tall(w_o, (t * 2 + 2 + s) * P))

            def up_rows(t, misc):
                if misc is not None:
                    hold(p_m, misc)
                for h in range(2):
                    col = ds(t * P + h * FF, P)
                    sp.dma_start(fr[0:16, h, :], st_f[:, col]).then_inc(cwr_in, 16)
                    sp.dma_start(fr[16:19, h, :], wf[:, col]).then_inc(cwr_in, 16)
                    sp.dma_start(fr[19:20, h, :], inp["b_conv_f"][:, col]).then_inc(cwr_in, 16)

            mf = Count()
            mf.base = 2 + NC4 * PM_ITER
            load(tall(w_up, 0))
            load(tall(w_up, FF))
            hold(d_r, 3 * NG)
            up_rows(0, None)
            load(tall(w_up, P))
            load(tall(w_up, P + FF))
            up_rows(1, mf.at(1))

            def ffn(t, last):
                load(tall(w_up, (2 * t) * P))
                load(tall(w_up, (2 * t) * P + FF))
                up_rows(2 * t, mf.at(2))
                load(wide(w_down, 2 * t - 2, 0))
                load(wide(w_down, 2 * t - 2, 512))
                load(tall(w_up, (2 * t + 1) * P))
                load(tall(w_up, (2 * t + 1) * P + FF))
                up_rows(2 * t + 1, mf.at(4))
                mf.step(4)

            with loop(sp, 10, {job: 6, mf: 4}) as t:
                ffn(t + 1, False)
            sp.dma_start(pn[:, 0:BLK, :], pp).then_inc(p_in, 16)
            sp.dma_start(pn[0:NS, BLK, :], psm).then_inc(p_in, 16)
            load(wide(w_down, 20, 0))
            load(wide(w_down, 20, 512))
            load(wide(w_ple, 0, 0))
            load(wide(w_ple, 0, 512))
            load(tall(w_gate, 0))
            load(tall(w_gate, P))
            with loop(sp, 3, {job: 2}) as t:
                for s in range(2):
                    load(tall(w_gate, (t * 2 + 2 + s) * P))
            assert job.base == NJOBS, job.base
            hold(y_out[0], 16 * 3)
            hold(y_out[1], 16)
            hold(so_out, 16 * (NC4 * 2 + 22 * 4))

        @block.gpsimd
        def _(pool):
            me = Count()

            def then(ins):
                ins.then_inc(g_self, 1)
                pool.wait_ge(g_self, me.step())

            g = nc.gpsimd
            then(g.memset(ident[:, :], 0.0))
            g.affine_select(out=ident[:, :], in_=ident[:, :], compare_op=ALU.not_equal, fill=1.0, base=0,
                            pattern=[[-1, P]], channel_multiplier=1).then_inc(g_const, 1)
            then(g.memset(ones[:, :], 1.0))
            then(g.memset(eps[:, :], EPS))
            g.affine_select(out=trif[:, :], in_=ones[:, :], compare_op=ALU.is_ge, fill=0.0, base=0,
                            pattern=[[-1, P]], channel_multiplier=1)
            g.affine_select(out=compf[:, :], in_=ones[:, :], compare_op=ALU.is_gt, fill=0.0, base=0,
                            pattern=[[1, P]], channel_multiplier=-1)
            then(g.memset(far[:, :], 0.0))
            g.affine_select(out=far[:, :], in_=far[:, :], compare_op=ALU.is_gt, fill=FAR, base=0,
                            pattern=[[1, P]], channel_multiplier=-1)
            then(g.memset(fars[:, :], 0.0))
            new = fars[:, 0:P].rearrange("p (b h q) -> p b h q", b=NB, h=2)
            then(g.affine_select(out=new, in_=new, compare_op=ALU.is_gt, fill=FAR, base=0,
                                 pattern=[[NT, NB], [0, 2], [1, NT]], channel_multiplier=-1))
            g.affine_select(out=new, in_=new, compare_op=ALU.is_ge, fill=FAR, base=0,
                            pattern=[[-NT, NB], [0, 2], [0, NT]], channel_multiplier=1)
            g.memset(qbd[:, :, :, :], 0.0).then_inc(g_const, 1)

            job = Count()
            rawn = [Count(), Count()]
            sqn = Count()

            def fold(gain):
                s = job.base % 2
                pool.wait_ge(raw_in[s], rawn[s].step(32))
                if gain is None:
                    pool.wait_ge(g_fold, job.at())
                    pool.sem_inc(g_fold, 1)
                else:
                    r = raw[s][:, :].rearrange("p (k n) -> p k n", n=P)
                    gv = gains[:, gain * KD:(gain + 1) * KD].unsqueeze(2).to_broadcast([P, KD, P])
                    g.tensor_tensor(r, r, gv, ALU.mult).then_inc(g_fold, 1)
                job.step()

            def add_square(gr):
                k = sqn.base
                if k:
                    pool.wait_ge(g_ss, sqn.at())
                pool.wait_ge(a_sq, sqn.step())
                w = GROUPS[gr][1]
                g.tensor_tensor(part(ss[:, :], gr), part(ss[:, :], gr), sq[k % 2][:, 0:w], ALU.add).then_inc(g_ss, 1)

            def clear_sums():
                then(g.memset(ss[:, :], 0.0))

            clear_sums()
            pool.wait_ge(a_m, 1)
            fold(0)
            fold(0)
            for gr in range(NG):
                for k in range(KD):
                    add_square(gr)
            with loop(pool, NC4 - 1, {job: NIN, rawn[0]: 16 * NIN, rawn[1]: 16 * NIN}):
                for n in range(NIN):
                    fold(0)
            for n in range(NIN - 2):
                fold(0)
            with loop(pool, 4, {job: 2, rawn[0]: 32, rawn[1]: 32}):
                fold(None)
                fold(None)
            fold(None)
            fold(None)
            pool.wait_ge(d_mrg, 8 * NG)
            clear_sums()
            with loop(pool, 3, {job: 2, rawn[0]: 32, rawn[1]: 32, sqn: 6}):
                for s in range(2):
                    for gr in range(NG):
                        add_square(gr)
                    fold(None)
            for s in range(2):
                for gr in range(NG):
                    add_square(gr)
                fold(2)
            pool.wait_ge(d_r, 2 * NG)
            clear_sums()
            for gr in range(NG):
                for k in range(KD):
                    add_square(gr)
            pool.wait_ge(d_xlo, 8 + 24)
            g.memset(y[:, :, :], 0.0).then_inc(g_acc0, 1)
            pool.wait_ge(d_r, 3 * NG)
            clear_sums()
            fold(2)
            fold(2)
            with loop(pool, 10, {job: 6, rawn[0]: 96, rawn[1]: 96}):
                fold(2)
                fold(2)
                fold(None)
                fold(None)
                fold(2)
                fold(2)
            fold(None)
            fold(None)
            fold(None)
            for m in range(KD):
                for gr in range(NG):
                    add_square(gr)
                if m == 3:
                    fold(None)
            pool.wait_ge(d_r, 4 * NG)
            clear_sums()
            fold(4)
            fold(4)
            xln = Count()

            def add_low(gr, k):
                pool.wait_ge(d_t, 24 + xln.step())
                g.tensor_tensor(part(y[:, k, :], gr), part(y[:, k, :], gr), part(f(bl[:, k, :]), gr), ALU.add).then_inc(g_xl, 1)

            order = [(gr, k) for gr in range(NG) for k in range(KD)]
            for i, (gr, k) in enumerate(order):
                add_low(gr, k)
                if i >= 2:
                    add_square(order[i - 2][0])
            add_square(NG - 1)
            add_square(NG - 1)
            pool.wait_ge(d_r, 5 * NG)
            clear_sums()
            with loop(pool, 3, {job: 2, rawn[0]: 32, rawn[1]: 32, sqn: 6}):
                for s in range(2):
                    fold(4)
                    for gr in range(NG):
                        add_square(gr)
            for s in range(2):
                for gr in range(NG):
                    add_square(gr)
            for gr, k in order:
                add_low(gr, k)
            assert job.base == NJOBS, job.base

        @block.scalar
        def _(act):
            s_ = nc.scalar
            me = Count()
            job, unit, sqn, mis, rtn = Count(), Count(), Count(), Count(), Count()
            xhn = Count()

            def then(ins):
                ins.then_inc(a_self, 1)
                act.wait_ge(a_self, me.step())

            fld = Count()

            def ends(j):
                if fld.turn is None:
                    return ENDS[j]
                n, per = turn_jobs
                return ENDS[j + n] - per + fld.turn

            def whi():
                s = job.base % 2
                act.wait_ge(g_fold, job.at(1))
                if job.base >= 2:
                    act.wait_ge(p_unit, ends(job.base - 2))
                s_.activation(wh[s][:, :], raw[s][:, :], ACT.Copy).then_inc(a_hi, 1)
                job.step()

            pmn = Count()

            def evac(ops, done=None):
                b = mb_[mis.base % 2]
                mis.step()
                if done is None:
                    act.wait_ge(p_m, pmn.step())
                else:
                    act.wait_ge(p_av, done)
                for i, (dst, src) in enumerate(ops(b)):
                    ins = s_.activation(dst, src, ACT.Copy)
                ins.then_inc(a_m, 1)

            def square(src, gr):
                k = sqn.base
                if k >= 2:
                    act.wait_ge(g_ss, sqn.at(-1))
                sqn.step()
                s_.activation(sq[k % 2][:, 0:GROUPS[gr][1]], src, ACT.Square).then_inc(a_sq, 1)

            def rsqrt():
                for gr in range(NG):
                    act.wait_ge(d_unit, unit.step())
                    then(s_.activation(part(rt[:, :], gr), part(ms[:, :], gr), ACT.Ln))
                    s_.activation(part(rt[:, :], gr), part(rt[:, :], gr), ACT.Exp, scale=-0.5).then_inc(a_rt, 1)

            def tables(name):
                s_.preload_act_table_set(name)

            tables("natural_log_exp_and_others")
            evac(lambda b: [(gains[:, :], b[:, 0:6 * KD])])
            evac(lambda b: [(bias[:, :], b[:, 0:8])])
            whi()
            for gr in range(NG):
                for k in range(KD):
                    act.wait_ge(p_unit, unit.step())
                    b = ub[(unit.base - 1) % 3][:, 0:GROUPS[gr][1]]
                    s_.activation(part(xh[:, k, :], gr), b, ACT.Copy)
                    square(b, gr)
            rsqrt()

            stn = [Count() for _ in range(NG)]
            vno, soo, att = Count(), Count(), Count()

            def pair(c, it):
                evac(lambda b: [(cwt[:, :], b[:, 0:19])])
                whi()
                evac(lambda b: [(pkT[:, 0:512], b[:, :])])
                whi()
                for q in range(1, 4):
                    evac(lambda b: [(pkT[:, q * 512:(q + 1) * 512], b[:, :])])
                whi()
                for kind in range(2):
                    for g in range(NG):
                        if kind == 0:
                            act.wait_ge(stg_out[g], stn[g].at())
                            dst = stg[g][:, :].rearrange("p (b n) -> p b n", n=P)
                        else:
                            if g == 0:
                                act.wait_ge(vn_out, vno.at())
                            dst = vn[:, 3 * g:3 * g + 3, :]

                        def ops(b, dst=dst, g=g):
                            b = b[:, 0:384].rearrange("p (b n) -> p b n", n=P)
                            if g < 2:
                                return [(dst, b)]
                            return [(dst[:, 0:2, :], b[:, 0:2, :]), (dst[0:NS, 2, :], b[0:NS, 2, :])]
                        evac(ops)
                        act.wait_ge(a_m, mis.at())
                        o, os_, sm = (kp_o, ks_o, stg_out[g]) if kind == 0 else (vp_o, vs_o, vn_out)
                        nb = 3 if g < 2 else 2
                        act.dma_start(o[:, 3 * g:3 * g + nb, ds(c * P, P)], dst[:, 0:nb, :]).then_inc(sm, 16)
                        if g == 2:
                            act.dma_start(os_[:, ds(c * P, P)], dst[0:NS, 2, :]).then_inc(sm, 16)
                        if kind == 0:
                            stn[g].step(16 if g < 2 else 32)
                for g in range(NG):
                    stn[g].step(64)
                vno.step(64)

                for n in range(SLOTS):
                    if n >= 1 and n - 1 < NSTEP:
                        s = n - 1
                        w = step_shape(s)[1]
                        act.wait_ge(d_sp, att.at(s + 1))
                        if s < 2:
                            act.wait_ge(p_tri, att.at(0))
                        elif s - 2 in COMPS:
                            act.wait_ge(p_comp, cmp.at(COMPS.index(s - 2) + 1))
                        else:
                            act.wait_ge(p_tri, att.at(s - 1))
                        s_.activation(lh[s % 2][:, 0:w], tt[s % 2][:, 0:w], ACT.Copy).then_inc(a_lhi, 1)
                    if n >= 2 and n - 2 < NSTEP:
                        s = n - 2
                        w = step_shape(s)[1]
                        act.wait_ge(d_sub, att.at(s + 1))
                        act.wait_ge(p_av, att.at(max(0, s - 1)))
                        s_.activation(aa[s % 2][:, 0:w], z[s % 3][:, 0:w], ACT.Exp).then_inc(a_a, 1)
                    if n < NSTEP:
                        act.wait_ge(d_z, att.at(n + 1))
                        act.wait_ge(d_llo, att.at(max(0, n - 1)))
                        w = step_shape(n)[1]
                        t = tt[n % 2][:, 0:w]
                        s_.activation(t, z[n % 3][:, 0:w], ACT.Abs).then_inc(a_abs, 1)
                        act.wait_ge(a_abs, att.at(n + 1))
                        s_.activation(t, t, ACT.Exp, scale=-1.0).then_inc(a_exp, 1)
                        act.wait_ge(a_exp, att.at(n + 1))
                        s_.activation(t, t, ACT.Ln, bias=1.0).then_inc(a_ln, 1)
                    if FILL_AT.get(n, 1) % 3 == 0:
                        whi()
                    if n >= 3 and step_shape(n - 3)[4]:
                        s = n - 3
                        if s == SAMPLE:
                            def ops(b):
                                src = b[:, 0:P].rearrange("p (b h q) -> p b h q", b=NB, h=2)
                                r = []
                                for h in range(2):
                                    rows = slice(64 * h, 64 * h + 64)
                                    r.append((oT[rows, ds(c, 1), SEQ:TOK].rearrange("p o (b q) -> p (o b) q", q=NT), src[rows, :, h, :]))
                                return r
                        else:
                            h, qh, _ = STEPS[s]

                            def ops(b, h=h, qh=qh):
                                rows = slice(64 * h, 64 * h + 64)
                                return [(oT[rows, ds(c, 1), qh * 512:qh * 512 + 512].rearrange("p o t -> p (o t)"), b[rows, :])]
                        evac(ops, att.at(s + 1))
                att.step(NSTEP)
                cmp.step(len(COMPS))
                fld.step(3 * NIN)
                act.wait_ge(so_out, soo.at())
                evac(lambda b: [(sot[0:2, 0, :], b[0:2, 0:P])])
                act.wait_ge(a_m, mis.at())
                act.dma_start(cp_o[:, ds(c * P, P)], sot[0:2, 0, :]).then_inc(so_out, 16)
                evac(lambda b: [(sot[:, 1, :], b[0:2 * NB, 0:P])])
                act.wait_ge(a_m, mis.at())
                act.dma_start(cs_o[:, ds(c * P, P)], sot[:, 1, :]).then_inc(so_out, 16)
                soo.step(32)

            cmp = Count()
            turn_jobs = (NIN, 3 * NIN)
            with loop(act, NC4, {fld: 3 * NIN, job: NIN, mis: M_ITER, pmn: PM_ITER, att: NSTEP, cmp: len(COMPS), stn[0]: 80, stn[1]: 80,
                                 stn[2]: 96, vno: 64, soo: 32}) as c:
                pair(c, None)
            unit.base += 3 * NIN * NC4

            act.wait_ge(p_unit, ENDS[39])
            act.wait_ge(d_unit, ENDS[39])
            for src, dst in ((cout, ch), (oT, oh)):
                for k in range(NC4):
                    s_.activation(dst[:, k, :], src[:, k, :], ACT.Copy).then_inc(a_xhi, 1)
                    xhn.step()

            gn = [Count(), Count()]
            mrg = Count()
            tables("sigmoid_and_others")

            def merge(s):
                act.wait_ge(gat_in[s], gn[s].step(32))
                for h in range(2):
                    s_.activation(gat[2 * s + h][:, :], gat[2 * s + h][:, :], ACT.Sigmoid).then_inc(a_sig, 1)

            def merge_hi(m):
                for gr in range(NG):
                    act.wait_ge(d_x, mrg.step())
                    s_.activation(part(bh[:, ds(m, 1), :].rearrange("p o t -> p (o t)"), gr), ma[gr][:, 0:GROUPS[gr][1]],
                                  ACT.Copy).then_inc(a_xhi, 1)
                    xhn.step()

            turn_jobs = (2, 12)
            with loop(act, 4, {fld: 12, job: 2, mrg: 6, xhn: 6, gn[0]: 32, gn[1]: 32}) as t:
                for s in range(2):
                    whi()
                    merge(s)
                    merge_hi(t * 2 + s)
                fld.step(12)
            unit.base += 48

            def squares(m):
                for gr in range(NG):
                    act.wait_ge(d_unit, unit.step())
                    square(part(y[:, ds(m, 1), :].rearrange("p o t -> p (o t)"), gr), gr)

            tables("natural_log_exp_and_others")
            act.wait_ge(d_mrg, 8 * NG)
            turn_jobs = (2, 6)
            with loop(act, 4, {fld: 6, job: 2, unit: 6, sqn: 6}) as t:
                for s in range(2):
                    whi()
                    squares(t * 2 + s)
                fld.step(6)
            rsqrt()
            dxn = Count()
            dxn.base = 8 * NG

            def update(done, n):
                for gr in range(NG):
                    for k in range(KD):
                        act.wait_ge(done, n.step())
                        s_.activation(part(bh[:, k, :], gr), part(y[:, k, :], gr), ACT.Copy).then_inc(a_xhi, 1)
                        xhn.step()
                        square(part(y[:, k, :], gr), gr)

            update(d_unit, unit)
            rsqrt()

            cgn, acn = Count(), Count()

            def rows(pr):
                evac(lambda b: [(fw[pr][:, :, :], b[:, 0:40].rearrange("p (h n) -> p h n", h=2))])

            def gelu():
                act.wait_ge(d_cg, cgn.step())
                s_.activation(cg[:, :], cg[:, :], ACT.Gelu_apprx_tanh).then_inc(a_gelu, 1)

            def act_hi(k):
                act.wait_ge(d_act, acn.step())
                s_.activation(fh[:, k, :], cg[:, :], ACT.Copy).then_inc(a_xhi, 1)
                xhn.step()

            def states(t):
                act.wait_ge(so_out, soo.at())
                evac(lambda b: [(fsot[:, :, :], b[0:18, 0:2 * P].rearrange("r (h n) -> r h n", h=2))])
                act.wait_ge(a_m, mis.at())
                for h in range(2):
                    act.dma_start(fp_o[:, ds(t * P + h * FF, P)], fsot[0:2, h, :]).then_inc(so_out, 16)
                    act.dma_start(fs_o[:, ds(t * P + h * FF, P)], fsot[2:18, h, :]).then_inc(so_out, 16)
                soo.step(64)

            def ffn(t, first):
                rows(0)
                whi()
                if not first:
                    states(t * 2 - 1)
                whi()
                gelu()
                if not first:
                    whi()
                    whi()
                    act.wait_ge(p_unit, unit.at(30))
                act_hi(0)
                rows(1)
                whi()
                states(t * 2)
                whi()
                gelu()
                act_hi(1)
                unit.step(12 if first else 36)
                if not first:
                    fld.step(36)

            tables("gelu_apprx_tanh_and_others")
            ffn(0, True)
            turn_jobs = (6, 36)
            with loop(act, 10, {fld: 36, unit: 36, job: 6, mis: 4, pmn: 4, cgn: 2, acn: 2, soo: 128, xhn: 2}) as t:
                ffn(t + 1, False)
            states(NFF - 1)
            act.wait_ge(so_out, soo.at())
            tables("natural_log_exp_and_others")
            whi()
            for m in range(KD):
                if m == 4:
                    whi()
                for gr in range(NG):
                    act.wait_ge(d_unit, unit.step())
                    square(part(y[:, m, :], gr), gr)
            rsqrt()
            for i in range(6):
                act.wait_ge(p_unit, unit.step())
                gr, k = i // 2, i % 2
                s_.activation(part(ph[:, k, :], gr), ub[(unit.base - 1) % 3][:, 0:GROUPS[gr][1]], ACT.Copy).then_inc(a_xhi, 1)
                xhn.step()
            whi()
            unit.base += 24
            whi()
            update(d_x, dxn)
            rsqrt()

            en, sg = Count(), Count()
            tables("sigmoid_and_others")

            def gate(m):
                for gr in range(NG):
                    act.wait_ge(d_unit, unit.step())
                    t = tmp[gr][:, 0:GROUPS[gr][1]]
                    s_.activation(t, t, ACT.Sigmoid).then_inc(a_sig, 1)
                    act.wait_ge(d_e, en.step())
                    square(part(y[:, ds(m, 1), :].rearrange("p o t -> p (o t)"), gr), gr)

            turn_jobs = (2, 6)
            with loop(act, 3, {fld: 6, job: 2, unit: 6, sqn: 6, en: 6}) as t:
                for s in range(2):
                    whi()
                    gate(t * 2 + s)
                fld.step(6)
            whi()
            gate(6)
            gate(7)
            tables("natural_log_exp_and_others")
            rsqrt()
            assert job.base == NJOBS, job.base
            for gr in range(NG):
                act.wait_ge(d_unit, unit.step(8))
                nb = 3 if gr < 2 else 2
                act.dma_start(yp_o[:, 3 * gr:3 * gr + nb, :], on[:, gr % 2, 0:nb, :]).then_inc(y_out[0 if gr != 1 else 1], 16)
                if gr == 2:
                    act.dma_start(ys_o, on[0:NS, 0, 2, :]).then_inc(y_out[0], 16)

        @block.vector
        def _(dve):
            v = nc.vector
            me = Count()
            job, unit, rtn, xhn = Count(), Count(), Count(), Count()

            def then(ins):
                ins.then_inc(d_self, 1)
                dve.wait_ge(d_self, me.step())

            def wlo():
                s = job.base % 2
                dve.wait_ge(a_hi, job.step())
                v.tensor_tensor(wl[s][:, :], raw[s][:, :], f(wh[s][:, :]), ALU.subtract).then_inc(d_lo, 1)

            def bank(gr):
                u = unit.base
                dve.wait_ge(p_unit, unit.step())
                return ub[u % 3][:, 0:GROUPS[gr][1]]

            def rstat():
                for gr in range(NG):
                    b = bank(gr)
                    v.tensor_scalar(part(ms[:, :], gr), b, 1.0 / D, EPS, ALU.mult, ALU.add).then_inc(d_unit, 1)
                dve.wait_ge(d_unit, unit.at())
                for gr in range(NG):
                    dve.wait_ge(a_rt, rtn.step())
                    r0, t, m, r = (part(x[:, :], gr) for x in (rt, t1, ms, rs))
                    then(v.tensor_tensor(t, r0, r0, ALU.mult))
                    then(v.scalar_tensor_tensor(out=t, in0=t, scalar=-0.5, in1=m, op0=ALU.mult, op1=ALU.mult))
                    v.scalar_tensor_tensor(out=r, in0=t, scalar=1.5, in1=r0, op0=ALU.add, op1=ALU.mult).then_inc(d_r, 1)
                dve.wait_ge(d_r, rtn.at())

            dve.wait_ge(g_const, 2)
            v.tensor_copy(tri[:, :], trif[:, :])
            v.tensor_copy(comp[:, :], compf[:, :])
            v.tensor_copy(full[:, :], ones[:, :]).then_inc(d_const, 1)
            wlo()
            for gr in range(NG):
                for k in range(KD):
                    b = bank(gr)
                    dve.wait_ge(a_sq, unit.at())
                    v.tensor_tensor(part(xl[:, k, :], gr), b, part(f(xh[:, k, :]), gr), ALU.subtract).then_inc(d_unit, 1)
            rstat()

            pm, mis, att, stn, son = Count(), Count(), Count(), [Count() for _ in range(NG)], Count()
            cmp = Count()

            def scaled(dst, b, gr):
                v.tensor_tensor(dst, b, part(rs[:, :], gr), ALU.mult).then_inc(d_unit, 1)

            def conv(src, dsts, w, bcol, done):
                views = [(lambda j: src[:, j:j + SEQ], dsts[0]),
                         (lambda j: src[:, US:UW].rearrange("p (b t) -> p b t", t=NT + 2)[:, :, j:j + NT], dsts[1])]
                for j in range(3):
                    for i, (xv, d) in enumerate(views):
                        if j == 0 and bcol is None:
                            ins = v.tensor_scalar(d, xv(0), w[0], None, ALU.mult)
                        elif j == 0:
                            ins = v.tensor_scalar(d, xv(0), w[0], bcol, ALU.mult, ALU.add)
                        else:
                            ins = v.scalar_tensor_tensor(out=d, in0=xv(j), scalar=w[j], in1=d, op0=ALU.mult, op1=ALU.add)
                        if j == 2 and i == 1 and done is not None:
                            ins.then_inc(done, 1)
                        elif i == 1:
                            then(ins)
                        yield

            def split_cols(t):
                return t[:, 0:SEQ], t[:, SEQ:TOK].rearrange("p (b t) -> p b t", t=NT)

            def pair(c):
                v.tensor_copy(bias2[:, 0:2], bias[:, ds(c * 2, 2)])
                then(v.tensor_scalar(bias2[:, 2:4], bias[:, ds(c * 2, 2)], 1 / SCALE, None, ALU.mult))
                mv = fars[:, :].rearrange("p (n h q) -> p n h q", h=2, q=NT)
                bv = bfars[:, :].rearrange("p (n h q) -> p n h q", h=2, q=NT)
                for h in range(2):
                    then(v.tensor_scalar(bv[:, :, h, :], mv[:, :, h, :], bias2[:, 2 + h:3 + h], None, ALU.add))
                wlo()
                for gr in range(NG):
                    scaled(part(qT[:, :], gr), bank(gr), gr)
                dve.wait_ge(d_unit, unit.at())
                for h in range(2):
                    rows = slice(64 * h, 64 * h + 64)
                    ins = v.tensor_copy(qbd[rows, :, h, :], qT[rows, SEQ:TOK].rearrange("p (b q) -> p b q", q=NT))
                ins.then_inc(d_qbd, 1)
                wlo()
                for gr in range(NG):
                    scaled(part(kT[:, :], gr), bank(gr), gr)
                wlo()
                dve.wait_ge(p_m, pm.at(5))
                for gr in range(NG):
                    scaled(part(vT[:, :], gr), bank(gr), gr)
                v.memset(uc[:, 0:2], 0.0)
                us = uc[:, US:UW].rearrange("p (b t) -> p b t", t=NT + 2)
                dve.wait_ge(a_m, mis.at(1))
                v.tensor_copy(us[:, :, 0:2], cwt[:, 0:16].rearrange("p (b t) -> p b t", t=2))

                taps = []

                def fill(i):
                    kind, gr = i // 3, i % 3
                    w = GROUPS[gr][1]
                    if kind == 2:
                        for _ in taps.pop() if taps else ():
                            pass
                    b = bank(gr)
                    if kind == 0:
                        for j, (d, cols) in enumerate(padded(uc, gr)):
                            ins = v.tensor_tensor(d, like(b[:, cols], d), like(part(rs[:, :], gr)[:, cols], d), ALU.mult)
                        ins.then_inc(d_unit, 1)
                    elif kind == 1:
                        scaled(tm1[:, 0:w], b, gr)
                        dve.wait_ge(d_unit, unit.at())
                        for d, cols in padded(uc, gr):
                            then(v.tensor_tensor(d, like(tm1[:, 0:w][:, cols], d), d, ALU.mult))
                        if gr == 2:
                            cc = cout[:, ds(c, 1), :].rearrange("p o t -> p (o t)")
                            wts = [cwt[:, 16 + j:17 + j] for j in range(3)]
                            dve.wait_ge(p_m, pm.at(0))
                            v.tensor_copy(so[:, 0:2], uc[:, SEQ:SEQ + 2])
                            v.tensor_copy(so[:, 2:18].rearrange("p (b t) -> p b t", t=2), us[:, :, NT:NT + 2]).then_inc(d_so, 1)
                            taps.append(conv(uc, split_cols(cc), wts, None, None))
                    elif kind == 2:
                        scaled(tm1[:, 0:w], b, gr)
                        dve.wait_ge(d_unit, unit.at())
                        cc = part(cout[:, ds(c, 1), :].rearrange("p o t -> p (o t)"), gr)
                        then(v.tensor_tensor(cc, cc, tm1[:, 0:w], ALU.mult))
                    else:
                        dve.wait_ge(stg_out[gr], stn[gr].at((16 if gr < 2 else 32) + 16 * (kind - 3)))
                        scaled(stg[gr][:, 0:w], b, gr)

                for n in range(SLOTS):
                    if n >= 1 and n - 1 < NSTEP:
                        s = n - 1
                        w = step_shape(s)[1]
                        dve.wait_ge(a_ln, att.at(s + 1))
                        t = tt[s % 2][:, 0:w]
                        v.scalar_tensor_tensor(out=t, in0=z[s % 3][:, 0:w], scalar=0.0, in1=t, op0=ALU.max, op1=ALU.add).then_inc(d_sp, 1)
                    if n >= 2 and n - 2 < NSTEP:
                        s = n - 2
                        o, w = step_shape(s)[:2]
                        dve.wait_ge(p_tri, att.at(s + 1))
                        v.tensor_tensor(z[s % 3][:, 0:w], z[s % 3][:, 0:w], pb_[:, o:o + w], ALU.subtract).then_inc(d_sub, 1)
                    if n < NSTEP:
                        w = step_shape(n)[1]
                        dve.wait_ge(p_s, att.at(n + 1))
                        dve.wait_ge(a_a, att.at(max(0, n - 2)))
                        off = bias2[:, STEPS[n][0]:STEPS[n][0] + 1] if n < SAMPLE else 0.0
                        v.tensor_scalar(z[n % 3][:, 0:w], sb_[n % 2][:, 0:w], SCALE, off, ALU.mult, ALU.add).then_inc(d_z, 1)
                    i = FILL_AT.get(n)
                    if i is not None and i % 3 == 0:
                        wlo()
                    if n >= 1 and n - 1 < NSTEP:
                        s = n - 1
                        w = step_shape(s)[1]
                        dve.wait_ge(a_lhi, att.at(s + 1))
                        v.tensor_tensor(ll[s % 2][:, 0:w], tt[s % 2][:, 0:w], f(lh[s % 2][:, 0:w]), ALU.subtract).then_inc(d_llo, 1)
                    if i is not None:
                        fill(i)
                    for op in taps:
                        next(op, None)
                        next(op, None)
                att.step(NSTEP)
                mis.step(M_ITER)
                pm.step(PM_ITER)
                for gr in range(NG):
                    stn[gr].step(80 if gr < 2 else 96)

            mis.base = pm.base = 2
            with loop(dve, NC4, {job: NIN, unit: 3 * NIN, mis: M_ITER, pm: PM_ITER, att: NSTEP, stn[0]: 80, stn[1]: 80,
                                 stn[2]: 96, me: PAIR_SELF}) as c:
                pair(c)

            dve.wait_ge(d_self, me.at())
            for src, hi, lo in ((cout, ch, cl), (oT, oh, ol)):
                for k in range(NC4):
                    dve.wait_ge(a_xhi, xhn.step())
                    v.tensor_tensor(lo[:, k, :], src[:, k, :], f(hi[:, k, :]), ALU.subtract).then_inc(d_xlo, 1)

            sg, mg = Count(), Count()

            def merge(m, s):
                dve.wait_ge(d_mrg, mg.at())
                mg.step(NG)
                dve.wait_ge(a_sig, sg.at(1))
                for gr in range(NG):
                    b = bank(gr)
                    v.tensor_tensor(ma[gr][:, 0:GROUPS[gr][1]], b, part(gat[2 * s][:, :], gr), ALU.mult).then_inc(d_unit, 1)
                dve.wait_ge(a_sig, sg.at(2))
                sg.step(2)
                for gr in range(NG):
                    w = GROUPS[gr][1]
                    b = bank(gr)
                    v.tensor_tensor(mb[gr][:, 0:w], b, part(gat[2 * s + 1][:, :], gr), ALU.mult).then_inc(d_unit, 1)
                    dve.wait_ge(d_unit, unit.at())
                    v.tensor_tensor(ma[gr][:, 0:w], ma[gr][:, 0:w], mb[gr][:, 0:w], ALU.add).then_inc(d_x, 1)
                for gr in range(NG):
                    dve.wait_ge(a_xhi, xhn.step())
                    hi = part(bh[:, ds(m, 1), :].rearrange("p o t -> p (o t)"), gr)
                    lo = part(bl[:, ds(m, 1), :].rearrange("p o t -> p (o t)"), gr)
                    v.tensor_tensor(lo, ma[gr][:, 0:GROUPS[gr][1]], f(hi), ALU.subtract).then_inc(d_mrg, 1)

            with loop(dve, 4, {job: 2, unit: 12, xhn: 6, sg: 4, mg: 6}) as t:
                for s in range(2):
                    wlo()
                    merge(t * 2 + s, s)

            def plain(m):
                for gr in range(NG):
                    b = bank(gr)
                    v.tensor_copy(part(y[:, ds(m, 1), :].rearrange("p o t -> p (o t)"), gr), b).then_inc(d_unit, 1)

            with loop(dve, 4, {job: 2, unit: 6}) as t:
                for s in range(2):
                    wlo()
                    plain(t * 2 + s)
            rstat()

            tn = Count()

            def normed(gain, gr, k):
                yy = part(y[:, k, :], gr)
                col = gain * KD + k
                v.scalar_tensor_tensor(out=yy, in0=yy, scalar=gains[:, col:col + 1], in1=part(rs[:, :], gr),
                                       op0=ALU.mult, op1=ALU.mult).then_inc(d_t, 1)
                tn.step()

            def low(gr, k):
                dve.wait_ge(a_xhi, xhn.step())
                v.tensor_tensor(part(bl[:, k, :], gr), part(y[:, k, :], gr), part(f(bh[:, k, :]), gr), ALU.subtract).then_inc(d_xlo, 1)

            order = [(gr, k) for gr in range(NG) for k in range(KD)]
            for i, (gr, k) in enumerate(order):
                normed(1, gr, k)
                b = bank(gr)
                dve.wait_ge(d_t, tn.at())
                v.tensor_tensor(part(y[:, k, :], gr), part(y[:, k, :], gr), b, ALU.add).then_inc(d_unit, 1)
                if i >= 1:
                    low(*order[i - 1])
            low(*order[-1])
            rstat()

            mf = Count()
            mf.base = 2 + NC4 * M_ITER
            pmf = Count()
            pmf.base = 2 + NC4 * PM_ITER
            fln, gln, acn = Count(), Count(), Count()
            dve.wait_ge(g_acc0, 1)

            def states_in(pr, back):
                dve.wait_ge(a_m, mf.at(back))
                for h, u in enumerate((ug, uv)):
                    v.memset(u[:, 0:2], 0.0)
                    v.tensor_copy(u[:, US:UW].rearrange("p (b t) -> p b t", t=NT + 2)[:, :, 0:2],
                                  fw[pr][:, h, 0:16].rearrange("p (b t) -> p b t", t=2))

            def into(u):
                for gr in range(NG):
                    b = bank(gr)
                    for d, cols in padded(u, gr):
                        ins = v.tensor_tensor(d, like(b[:, cols], d), like(part(rs[:, :], gr)[:, cols], d), ALU.mult)
                    ins.then_inc(d_unit, 1)
                dve.wait_ge(d_unit, unit.at())

            def taps(pr, h):
                return [fw[pr][:, h, 16 + j:17 + j] for j in range(3)], fw[pr][:, h, 19:20]

            def conv_gate(pr):
                w, b = taps(pr, 0)
                return conv(ug, split_cols(cg), w, b, d_cg)

            def conv_val(pr):
                w, b = taps(pr, 1)
                yield from conv(uv, split_cols(cv), w, b, None)

            def states_out(back):
                dve.wait_ge(p_m, pmf.at(back))
                for h, u in enumerate((ug, uv)):
                    v.tensor_copy(fso[:, h, 0:2], u[:, SEQ:SEQ + 2])
                    ins = v.tensor_copy(fso[:, h, 2:18].rearrange("p (b t) -> p b t", t=2),
                                        u[:, US:UW].rearrange("p (b t) -> p b t", t=NT + 2)[:, :, NT:NT + 2])
                ins.then_inc(d_so, 1)

            def times():
                dve.wait_ge(a_gelu, gln.step())
                v.tensor_tensor(cg[:, :], cg[:, :], cv[:, :], ALU.mult).then_inc(d_act, 1)
                acn.step()

            def act_lo(k):
                dve.wait_ge(a_xhi, xhn.step())
                v.tensor_tensor(fl[:, k, :], cg[:, :], f(fh[:, k, :]), ALU.subtract).then_inc(d_xlo, 1)

            def down_unit(m, gr):
                b = bank(gr)
                yy = part(y[:, m, :], gr)
                v.tensor_tensor(yy, yy, b, ALU.add).then_inc(d_unit, 1)

            def ffn(first):
                wlo()
                states_in(0, 1)
                into(ug)
                wlo()
                for _ in conv_gate(0):
                    pass
                into(uv)
                states_out(0 if first else 2)
                cvg = conv_val(0)
                if not first:
                    for half in range(2):
                        wlo()
                        for i in range(12):
                            down_unit(4 * half + i // 3, i % 3)
                            if i % 4 == 3:
                                next(cvg)
                for _ in cvg:
                    pass
                times()
                act_lo(0)
                wlo()
                states_in(1, 2 if first else 3)
                into(ug)
                wlo()
                for _ in conv_gate(1):
                    pass
                into(uv)
                states_out(3 if first else 4)
                for _ in conv_val(1):
                    pass
                times()
                act_lo(1)
                mf.step(3 if first else 4)
                pmf.step(3 if first else 4)

            ffn(True)
            with loop(dve, 10, {job: 6, unit: 36, mf: 4, pmf: 4, gln: 2, acn: 2, xhn: 2, me: FFN_SELF}) as t:
                ffn(False)
            for half in range(2):
                wlo()
                for i in range(12):
                    down_unit(4 * half + i // 3, i % 3)
            rstat()
            for i in range(6):
                gr, k = i // 2, i % 2
                b = bank(gr)
                dve.wait_ge(a_xhi, xhn.step())
                v.tensor_tensor(part(pl[:, k, :], gr), b, part(f(ph[:, k, :]), gr), ALU.subtract).then_inc(d_unit, 1)
            for m in range(KD):
                if m % 4 == 0:
                    wlo()
                for gr in range(NG):
                    b = bank(gr)
                    v.tensor_copy(part(ple[:, m, :], gr), b).then_inc(d_unit, 1)

            xln = Count()
            order = [(gr, k) for gr in range(NG) for k in range(KD)]

            def residual(gain, after, split):
                for i in range(len(order) + 2):
                    if i < len(order):
                        normed(gain, *order[i])
                    if 1 <= i <= len(order):
                        gr, k = order[i - 1]
                        dve.wait_ge(g_xl, xln.step())
                        yy = part(y[:, k, :], gr)
                        v.tensor_tensor(yy, yy, part(f(bh[:, k, :]), gr), ALU.add).then_inc(d_x, 1)
                    if i >= 2 and split:
                        low(*order[i - 2])

            residual(3, None, True)
            rstat()
            en, sgn = Count(), Count()
            sgn.base = 16

            def gate(m):
                for gr in range(NG):
                    w = GROUPS[gr][1]
                    scaled(tmp[gr][:, 0:w], bank(gr), gr)
                    dve.wait_ge(a_sig, sgn.step())
                    e = part(y[:, ds(m, 1), :].rearrange("p o t -> p (o t)"), gr)
                    v.tensor_tensor(e, tmp[gr][:, 0:w], part(ple[:, ds(m, 1), :].rearrange("p o t -> p (o t)"), gr),
                                    ALU.mult).then_inc(d_e, 1)

            with loop(dve, 3, {job: 2, unit: 6, sgn: 6}) as t:
                for s in range(2):
                    wlo()
                    gate(t * 2 + s)
            wlo()
            gate(6)
            gate(7)
            rstat()
            assert job.base == NJOBS, job.base

            def natural(i):
                gr, k = order[i]
                if k == 0 and gr == 2:
                    dve.wait_ge(y_out[0], 16)
                u = unit.base
                dve.wait_ge(p_unit, unit.step())
                b = ub[u % 3][:, 0:384].rearrange("p (b n) -> p b n", n=P)
                o = on[:, gr % 2, :, k * P:(k + 1) * P]
                if gr < 2:
                    v.tensor_copy(o, b).then_inc(d_unit, 1)
                else:
                    v.tensor_copy(o[:, 0:2, :], b[:, 0:2, :])
                    v.tensor_copy(o[0:NS, 2, :], b[0:NS, 2, :]).then_inc(d_unit, 1)

            for i in range(len(order) + 3):
                if i < len(order):
                    normed(5, *order[i])
                if 1 <= i <= len(order):
                    gr, k = order[i - 1]
                    dve.wait_ge(g_xl, xln.step())
                    yy = part(y[:, k, :], gr)
                    v.tensor_tensor(yy, yy, part(f(bh[:, k, :]), gr), ALU.add).then_inc(d_x, 1)
                if i >= 3:
                    natural(i - 3)

        @block.tensor
        def _(pe):
            t_ = nc.tensor
            job, unit, mis, att, cmp = Count(), Count(), Count(), Count(), Count()

            def free_bank():
                u = unit.base
                if u >= 3:
                    pe.wait_ge(d_unit, unit.at(-2))
                unit.step()
                return ub[u % 3]

            def products(gr, terms, last_of_job=False):
                b = free_bank()[:, 0:GROUPS[gr][1]]
                n = len(terms)
                for i, (h, l, xhi, xlo) in enumerate(terms):
                    t_.matmul(b, h, xhi, start=(i == 0), stop=False)
                    t_.matmul(b, h, xlo, start=False, stop=False)
                    ins = t_.matmul(b, l, xhi, start=False, stop=(i == n - 1))
                ins.then_inc(p_unit, 1)
                return ins

            def begin_job():
                pe.wait_ge(d_lo, job.step())

            def tall(s, k):
                return wh[s][:, k * P:(k + 1) * P], wl[s][:, k * P:(k + 1) * P]

            def tile(gr, s, hi, lo, ks=range(KD), k0=0):
                products(gr, [(*tall(s, k), part(hi[:, k - k0, :], gr), part(lo[:, k - k0, :], gr)) for k in ks])

            def stat():
                for gr in range(NG):
                    b = free_bank()[:, 0:GROUPS[gr][1]]
                    pe.wait_ge(g_ss, ssn.base - (8 * (NG - 1 - gr) if ssg[0] else 0))
                    t_.matmul(b, ones[:, :], part(ss[:, :], gr), start=True, stop=True).then_inc(p_unit, 1)

            ssn, ssg = Count(), [True]

            def misc():
                pe.wait_ge(a_m, mis.at(-1))
                b = mb_[mis.base % 2]
                mis.step()
                return b

            pe.wait_ge(g_const, 2)
            pe.wait_ge(const_in, 16 * 7)
            t_.transpose(mb_[0][:, 0:6 * KD], gnat[:, :], ident[0:6 * KD, 0:6 * KD]).then_inc(p_m, 1)
            t_.matmul(mb_[1][:, 0:8], ones[0:1, :], brow[:, :], start=True, stop=True).then_inc(p_m, 1)
            mis.base = 2

            def turned(b, src, rows=P):
                return t_.transpose(b, src, ident[0:rows, 0:rows])

            def x_turned(gr, k, nat, smp):
                b = free_bank()
                for j, bl_ in enumerate(group_blocks(gr)):
                    if bl_ < BLK:
                        ins = turned(b[:, j * P:(j + 1) * P], nat[:, bl_, k * P:(k + 1) * P])
                    else:
                        ins = turned(b[:, j * P:j * P + NS], smp[:, k * P:(k + 1) * P], NS)
                ins.then_inc(p_unit, 1)

            for gr in range(NG):
                pe.wait_ge(x_in[gr], 32 if gr == 2 else 16)
                for k in range(KD):
                    x_turned(gr, k, xn, xn[0:NS, BLK, :])
            ssn.step(24)
            stat()
            pe.wait_ge(d_const, 1)

            cwn, pkn, pvn, son, qn = Count(), [Count(), Count()], Count(), Count(), Count()

            def pair():
                u0 = unit.base
                b = misc()
                pe.wait_ge(cwr_in, cwn.step(32))
                pe.sem_inc(pe_held, 1)
                turned(b[:, 0:19], cwr[:, :], 19).then_inc(p_m, 1)

                def past(q):
                    b = misc()
                    pe.wait_ge(pk_in[q % 2], pkn[q % 2].step(64))
                    for i in range(4):
                        ins = turned(b[:, i * P:(i + 1) * P], pk[:, q % 2, i, :])
                    ins.then_inc(p_m, 1)

                def new_rows(src, u, gr):
                    pe.wait_ge(d_unit, unit.at(u + gr + 1 - (unit.base - u0)))
                    b = misc()
                    for j, bl_ in enumerate(group_blocks(gr)):
                        w = block_rows(bl_)
                        ins = turned(b[0:w, j * P:(j + 1) * P], src[:, bl_ * P:bl_ * P + w])
                    ins.then_inc(p_m, 1)

                begin_job()
                for gr in range(NG):
                    tile(gr, (job.base - 1) % 2, xh, xl)
                past(0)
                begin_job()
                for gr in range(NG):
                    tile(gr, (job.base - 1) % 2, xh, xl)
                    past(gr + 1)
                begin_job()
                for gr in range(NG):
                    tile(gr, (job.base - 1) % 2, xh, xl)
                    new_rows(kT, 3, gr)
                for gr in range(NG):
                    new_rows(vT, 6, gr)

                obank = {}

                def scores(s):
                    o, w, dg, first, last = step_shape(s)
                    b = sb_[s % 2]
                    pe.wait_ge(d_z, att.at(max(0, s - 1)))
                    if s < SAMPLE:
                        h, qh, kb = STEPS[s]
                        rows = slice(64 * h, 64 * h + 64)
                        q0 = qh * 512 + o
                        ins = t_.matmul(b[:, 0:w], kT[rows, kb * P:(kb + 1) * P], qT[rows, q0:q0 + w], start=True, stop=True)
                        if dg:
                            ins = t_.matmul(b[:, 0:P], ident[:, :], far[:, :], start=False, stop=True, skip_group_check=True)
                    else:
                        pe.wait_ge(d_qbd, qn.step())
                        flat = qbd[:, :, :, :].rearrange("p b h q -> p (b h q)")
                        t_.matmul(b[:, 0:384], ident[:, :], bfars[:, :], start=True, stop=True, skip_group_check=True)
                        t_.matmul(b[0:NS, 0:P], kT[:, SEQ:TOK], flat, start=False, stop=True, skip_group_check=True)
                        for e in range(PAGES * NB):
                            ins = t_.matmul(b[:, P + 16 * e:P + 16 * e + 16], pkT[:, e * P:(e + 1) * P],
                                            flat[:, 16 * (e % NB):16 * (e % NB) + 16], start=False, stop=True, skip_group_check=True)
                    ins.then_inc(p_s, 1)

                def both(out_, w_, s, a, b_, start):
                    t_.matmul(out_, w_[:, :], lh[s % 2][:, a:b_], start=start, stop=False, skip_group_check=True)
                    return t_.matmul(out_, w_[:, :], ll[s % 2][:, a:b_], start=False, stop=True, skip_group_check=True)

                def within(s):
                    o, w, dg, first, last = step_shape(s)
                    pe.wait_ge(d_llo, att.at(s + 1))
                    if first:
                        pe.wait_ge(d_sub, att.at(s))
                    if s < SAMPLE:
                        both(pb_[:, o:o + w], tri, s, 0, w, first).then_inc(p_tri, 1)
                    else:
                        for j in range(3):
                            c = pb_[:, j * P:(j + 1) * P]
                            ins = both(c, tri, s, j * P, (j + 1) * P, j == 0)
                            for i in range(j):
                                ins = both(c, full, s, i * P, (i + 1) * P, False)
                        ins.then_inc(p_tri, 1)

                def rest(s):
                    o, w, dg, first, last = step_shape(s)
                    pe.wait_ge(d_sub, att.at(s + 1))
                    both(pb_[:, o:o + w], comp, s, 0, w, False).then_inc(p_comp, 1)

                def values(s):
                    o, w, dg, first, last = step_shape(s)
                    pe.wait_ge(a_a, att.at(s + 1))
                    if first:
                        obank[0] = misc()
                    b = obank[0]
                    if s < SAMPLE:
                        kb = STEPS[s][2]
                        ins = t_.matmul(b[:, o:o + w], vn[:, kb, :], aa[s % 2][:, 0:w], start=first, stop=last, skip_group_check=True)
                    else:
                        pe.wait_ge(pv_in, pvn.step(256))
                        t_.matmul(b[:, 0:P], vn[0:NS, BLK, :], aa[s % 2][0:NS, 0:P], start=True, stop=False, skip_group_check=True)
                        for e in range(PAGES * NB):
                            c = 16 * (e % NB)
                            ins = t_.matmul(b[:, c:c + 16], pv[:, e, :], aa[s % 2][:, P + 16 * e:P + 16 * e + 16],
                                            start=False, stop=(e == PAGES * NB - 1), skip_group_check=True)
                    ins.then_inc(p_av, 1)

                def piece(i, k):
                    gr, s = i % 3, (job.base - (0 if i % 3 == 0 and k == 0 else 1)) % 2
                    if k == 0:
                        if gr == 0:
                            begin_job()
                        fbank[0] = free_bank()[:, 0:GROUPS[gr][1]]
                    (h, l), xhi, xlo, b = tall(s, k), part(xh[:, k, :], gr), part(xl[:, k, :], gr), fbank[0]
                    t_.matmul(b, h, xhi, start=(k == 0), stop=False, skip_group_check=True)
                    t_.matmul(b, h, xlo, start=False, stop=False, skip_group_check=True)
                    ins = t_.matmul(b, l, xhi, start=False, stop=(k == KD - 1), skip_group_check=True)
                    if k == KD - 1:
                        ins.then_inc(p_unit, 1)

                fbank = [None]
                for n in range(SLOTS):
                    if n < NSTEP:
                        scores(n)
                    if n >= 3:
                        values(n - 3)
                    for q in range(PIECES * n, PIECES * (n + 1)):
                        if q == PIECES * n + AHEAD and 0 <= n - 2 < NSTEP:
                            within(n - 2)
                        piece(*divmod(q, KD))
                    if n - 2 in COMPS:
                        rest(n - 2)
                att.step(NSTEP)
                cmp.step(len(COMPS))
                pe.wait_ge(d_so, son.step())
                turned(misc()[0:2, 0:P], so[:, 0:2]).then_inc(p_m, 1)
                turned(misc()[0:2 * NB, 0:P], so[:, 2:18]).then_inc(p_m, 1)

            with loop(pe, NC4, {job: NIN, unit: 3 * NIN, mis: M_ITER, att: NSTEP, cmp: len(COMPS), cwn: 32,
                                pkn[0]: 128, pkn[1]: 128, pvn: 256, son: 1, qn: 1}):
                pair()

            pe.wait_ge(d_xlo, 8)
            with loop(pe, 4, {job: 2, unit: 12}):
                for s in range(2):
                    begin_job()
                    for hi, lo, k0 in ((ch, cl, 0), (oh, ol, 4)):
                        for gr in range(NG):
                            tile(gr, s, hi, lo, range(k0, k0 + 4), k0)
            pe.wait_ge(d_mrg, 8 * NG)
            with loop(pe, 4, {job: 2, unit: 6}):
                for s in range(2):
                    begin_job()
                    for gr in range(NG):
                        tile(gr, s, bh, bl)
            ssn.step(24)
            ssg[0] = False
            stat()
            pe.wait_ge(x2_in, 32)
            for gr in range(NG):
                for k in range(KD):
                    x_turned(gr, k, xn2, xn2s)
            ssn.step(24)
            ssg[0] = True
            stat()

            xlo = Count()
            xlo.base = 8 + 24

            def down(s, half):
                begin_job()
                for m in range(4):
                    for gr in range(NG):
                        products(gr, [(wh[s][:, k * 512 + m * P:k * 512 + (m + 1) * P], wl[s][:, k * 512 + m * P:k * 512 + (m + 1) * P],
                                       part(fh[:, k, :], gr), part(fl[:, k, :], gr)) for k in range(2)])

            def rows_turned():
                b = misc()
                pe.wait_ge(cwr_in, cwn.step(96))
                pe.sem_inc(pe_held, 1)
                for h in range(2):
                    ins = turned(b[:, h * 20:h * 20 + 20], fr[:, h, :], 20)
                ins.then_inc(p_m, 1)

            def states_turned():
                pe.wait_ge(d_so, son.step())
                b = misc()
                for h in range(2):
                    ins = turned(b[0:18, h * P:(h + 1) * P], fso[:, h, :])
                ins.then_inc(p_m, 1)

            def up(states):
                rows_turned()
                for h in range(2):
                    if h and states:
                        states_turned()
                    begin_job()
                    for gr in range(NG):
                        tile(gr, (job.base - 1) % 2, bh, bl)

            def ffn(first):
                up(not first)
                if not first:
                    pe.wait_ge(d_xlo, xlo.at())
                    down(0, 0)
                    down(1, 1)
                up(True)
                xlo.step(2)

            pe.wait_ge(d_xlo, 8 + 24)
            ffn(True)
            with loop(pe, 10, {job: 6, unit: 36, mis: 4, cwn: 192, son: 2, xlo: 2}):
                ffn(False)
            states_turned()
            pe.wait_ge(d_xlo, xlo.at())
            down(0, 0)
            down(1, 1)
            ssn.step(24)
            ssg[0] = False
            stat()
            pe.wait_ge(p_in, 32)
            for gr in range(NG):
                for k in range(2):
                    x_turned(gr, k, pn, pn[0:NS, BLK, :])
            pe.wait_ge(d_unit, unit.at())
            for half in range(2):
                begin_job()
                for m in range(4):
                    for gr in range(NG):
                        products(gr, [(wh[half][:, k * 512 + m * P:k * 512 + (m + 1) * P], wl[half][:, k * 512 + m * P:k * 512 + (m + 1) * P],
                                       part(ph[:, k, :], gr), part(pl[:, k, :], gr)) for k in range(2)])
            ssn.step(24)
            ssg[0] = True
            stat()
            base = xlo.base
            pe.wait_ge(d_xlo, base + 24)
            with loop(pe, 4, {job: 2, unit: 6}):
                for s in range(2):
                    begin_job()
                    for gr in range(NG):
                        tile(gr, s, bh, bl)
            ssn.step(24)
            ssg[0] = False
            stat()
            dx = 8 * NG + 24
            for gr in range(NG):
                for k in range(KD):
                    dx += 1
                    b = free_bank()
                    pe.wait_ge(d_x, dx)
                    for j, bl_ in enumerate(group_blocks(gr)):
                        w = block_rows(bl_)
                        ins = turned(b[0:w, j * P:(j + 1) * P], y[:, k, bl_ * P:bl_ * P + w])
                    ins.then_inc(p_unit, 1)
            assert job.base == NJOBS, job.base


PAIR_SELF = 13
FFN_SELF = 10

_INS = ["x_prompt", "x_sample", "cache_k", "cache_v", "state_conv", "state_ffn_conv", "page_table", "p_prompt",
        "p_sample", "g_pre_mix", "w_in", "w_conv_a", "w_a", "w_b", "sb_bias", "w_o", "g_post_mix", "g_pre_ffn",
        "w_up", "w_conv_f", "b_conv_f", "w_down", "g_post_ffn", "w_ple", "g_ple_gate", "w_ple_gate", "g_post_ple"]
_OUTS = [("y_prompt", (1, SEQ, D)), ("y_sample", (NB, NT, D)),
         ("k_prompt", (1, 1, SEQ, 8, 64)), ("v_prompt", (1, 1, SEQ, 8, 64)),
         ("conv_prompt", (1, 1, 2, CW)), ("ffn_conv_prompt", (1, 1, 2, 2 * FF)),
         ("k_sample", (1, NB, NT, 8, 64)), ("v_sample", (1, NB, NT, 8, 64)),
         ("conv_sample", (1, NB, 2, CW)), ("ffn_conv_sample", (1, NB, 2, 2 * FF))]


def kernel(**inputs):
    import numpy as np
    import concourse.bacc as bacc
    from concourse.bass_utils import run_bass_kernel_spmd

    nc = bacc.Bacc("TRN2", target_bir_lowering=False, num_devices=1)
    arrays, inp, out = {}, {}, {}
    for name in _INS:
        arrays[f"in_{name}"] = np.ascontiguousarray(inputs[name])
        inp[name] = nc.dram_tensor(f"in_{name}", arrays[f"in_{name}"].shape, mybir.dt.from_np(arrays[f"in_{name}"].dtype),
                                   kind="ExternalInput").ap()
    for name, shape in _OUTS:
        out[name] = nc.dram_tensor(f"out_{name}", shape, F32, kind="ExternalOutput").ap()
    gate_spill = nc.dram_tensor("gate_spill", (2 * KD, P, TOK), F32).ap()
    build(nc, inp, out, gate_spill)
    got = run_bass_kernel_spmd(nc, [arrays], core_ids=[0]).results[0]
    return tuple(got[f"out_{name}"] for name, _ in _OUTS)
```

```python
from contextlib import ExitStack, contextmanager

import concourse.bass as bass
from concourse import mybir

F32 = mybir.dt.float32
F32R = mybir.dt.float32r
I32 = mybir.dt.int32
ALU = mybir.AluOpType
ACT = mybir.ActivationFunctionType
ds = bass.ds

P = 128
D = 1024
KD = D // P
SEQ = 1024
NB, NT = 8, 8
NS = NB * NT
TOK = SEQ + NS
GROUPS = [(0, 384), (384, 384), (768, 320)]
NG = 3
BLK = SEQ // P
CW = 512
NC4 = CW // P
FF = 2816
NFF = FF // P
PLE = 256
PAGES = 2
EPS = 1e-6
SCALE = 64 ** -0.5
FAR = -1.0e30 / SCALE
UW = SEQ + 2 + NB * (NT + 2)
US = SEQ + 2
GAINS = ["g_pre_mix", "g_post_mix", "g_pre_ffn", "g_post_ffn", "g_ple_gate", "g_post_ple"]

STEPS = [(h, qh, kb) for h in range(2) for qh in range(2) for kb in range(4 * qh + 3, -1, -1)]
NPS = len(STEPS)
NSTEP = NPS + 1
SAMPLE = NPS
SLOTS = NSTEP + 3
IN_FILL = 21
PIECES = IN_FILL * KD // SLOTS
assert PIECES * SLOTS == IN_FILL * KD
AHEAD = 1
FILL_AT = {(KD * i + KD - 1) // PIECES: i for i in range(IN_FILL)}
M_ITER = 18
PM_ITER = 13


def step_shape(s):
    if s == SAMPLE:
        return 0, 384, True, True, True
    h, qh, kb = STEPS[s]
    q0 = max(kb * P, qh * 512)
    return q0 - qh * 512, qh * 512 + 512 - q0, kb >= 4 * qh, kb == 4 * qh + 3, kb == 0


COMPS = [s for s in range(NSTEP) if not step_shape(s)[4]]


def job_ends():
    n, ends = KD * NG, []
    for units in ([3] * 40 + [6] * 8 + [3] * 8 + [(27, 3)] + [3] * 3 + [3, 3, 12, 12, 3, 3] * 10 + [12] * 2
                  + [(6, 12), (3, 12)] + [3] * 8):
        gap, k = units if isinstance(units, tuple) else (0, units)
        n += gap + k
        ends.append(n)
    return ends


ENDS = job_ends()
LAST_UP = NC4 * 10 + 8 + 8 + 4 + 60 - 1
WIDE0, WIDE1 = ENDS[NC4 * 10 + 16] - 3, ENDS[LAST_UP + 2]
XHI1 = 2 * NC4 + KD * NG
XHI2 = XHI1 + KD * NG + NFF + 2 * NG


class Count:

    def __init__(self):
        self.base, self.turn = 0, None

    def at(self, d=0):
        v = self.base + d
        return v if self.turn is None else v + self.turn

    def step(self, k=1):
        self.base += k
        return self.at()


@contextmanager
def loop(eng, n, adds):
    with eng.Fori(0, n) as it:
        before = {c: c.base for c in adds}
        for c, per in adds.items():
            c.turn = it * per
        yield it
        for c, per in adds.items():
            assert c.base - before[c] == per, (list(adds.values()), [x.base - before[x] for x in adds])
            c.turn = None
    for c, per in adds.items():
        c.base = before[c] + n * per


def build(nc, inp, out, gate_spill):
    with ExitStack() as ctx:
        def sem(name):
            return ctx.enter_context(nc.semaphore(name))

        BASE = 16512
        TOP = 229368

        def at(name, shape, offset, dt=F32):
            size = 4
            for x in shape[1:]:
                size *= x
            assert BASE + offset + size <= TOP, (name, offset + size)
            return nc.alloc_sbuf_tensor_at(name, shape, dt, offset=BASE + offset)

        class Region:
            def __init__(self, start, end):
                self.p, self.end = start, end

            def take(self, name, shape, dt=F32):
                size = 4
                for x in shape[1:]:
                    size *= x
                t = at(name, shape, self.p, dt)
                self.p += (size + 31) // 32 * 32
                assert self.p <= self.end, (name, self.p, self.end)
                return t

        ACTS = 8 * TOK * 4
        R1, R2, R3 = 0, 2 * ACTS, 4 * ACTS
        RTOP = TOP - BASE
        xh = at("xh", [P, KD, TOK], R1, F32R)
        xl = at("xl", [P, KD, TOK], R1 + ACTS, F32R)
        a = Region(R1, R2)
        ch, cl, oh, ol = (a.take(n, [P, NC4, TOK], F32R) for n in ("ch", "cl", "oh", "ol"))
        y = at("y", [P, KD, TOK], R1)
        xn2 = at("xn2", [P, BLK, D], R1 + ACTS)
        a = Region(R1 + ACTS, R2)
        fh, fl = a.take("fh", [P, 2, TOK], F32R), a.take("fl", [P, 2, TOK], F32R)
        pn = at("pn", [P, BLK + 1, PLE], R2 - 9 * PLE * 4)
        ple = at("ple", [P, KD, TOK], R1 + ACTS)
        on = at("on", [P, 2, 3, D], R1 + ACTS)
        xn = at("xn", [P, BLK + 1, D], R2)
        cout = at("cout", [P, NC4, TOK], R2)
        oT = at("oT", [P, NC4, TOK], R2 + NC4 * TOK * 4)
        bh = at("bh", [P, KD, TOK], R2, F32R)
        bl = at("bl", [P, KD, TOK], R2 + ACTS, F32R)
        xw = at("xw", [P, KD, TOK], R2 + ACTS)
        a = Region(R3, RTOP)
        raw = [a.take(f"raw{i}", [P, 1024]) for i in range(2)]
        wh = [a.take(f"wh{i}", [P, 1024], F32R) for i in range(2)]
        wl = [a.take(f"wl{i}", [P, 1024], F32R) for i in range(2)]
        rs = a.take("rs", [P, TOK])
        ident = a.take("ident", [P, P])
        ones = a.take("ones", [P, P])
        tri = a.take("tri", [P, P], F32R)
        comp = a.take("comp", [P, P], F32R)
        full = a.take("full", [P, P], F32R)
        far = a.take("far", [P, P])
        fars = a.take("fars", [P, 384])
        bfars = a.take("bfars", [P, 384])
        gains = a.take("gains", [P, 6 * KD])
        bias = a.take("bias", [P, 8])
        bias2 = a.take("bias2", [P, 8])
        qbd = a.take("qbd", [P, NB, 2, NT])
        R3T = a.p
        a = Region(R3T, RTOP)
        ss = a.take("ss", [P, TOK])
        sq = [a.take(f"sq{i}", [P, 384]) for i in range(2)]
        tmp = [a.take(f"tmp{i}", [P, 384]) for i in range(2)] + [at("tmp2", [P, 384], (RTOP - 384 * 4) // 32 * 32)]
        NORM = a.p
        ms, rt = (a.take(n, [P, TOK]) for n in ("ms", "rt"))
        xn2s = a.take("xn2s", [NS, D])
        trif, compf = a.take("trif", [P, P]), a.take("compf", [P, P])
        gnat = a.take("gnat", [6 * KD, P])
        brow = a.take("brow", [1, 8])
        a = Region(R2 + ACTS, R3)
        qT, kT, vT = (a.take(n, [P, TOK]) for n in ("qT", "kT", "vT"))
        pk = at("pk", [P, 2, 4, P], a.p - TOK * 4)
        vn = a.take("vn", [P, BLK + 1, P])
        pkT = a.take("pkT", [P, PAGES * NB * P])
        a2 = Region(R3T, RTOP)
        pv = a2.take("pv", [P, PAGES * NB, P])
        uc = a2.take("uc", [P, UW])
        tm1 = a.take("tm1", [P, 384])
        stg = [a2.take(f"stg{i}", [P, 384]) for i in range(NG)]
        z = [a2.take(f"z{i}", [P, 512]) for i in range(3)]
        tt = [a2.take(f"tt{i}", [P, 512]) for i in range(2)]
        lh = [a2.take(f"lh{i}", [P, 512], F32R) for i in range(2)]
        ll = [a2.take(f"ll{i}", [P, 512], F32R) for i in range(2)]
        aa = [a.take(f"aa{i}", [P, 512]) for i in range(2)]
        cwr = a.take("cwr", [2 * NB + 3, P])
        so = a.take("so", [P, 18])
        sot = a2.take("sot", [2 * NB, 2, P])
        cwt = a2.take("cwt", [P, 19])
        pgt = a.take("pgt", [1, NB * PAGES], I32)
        a = Region(R3T, RTOP)
        gat = [a.take(f"gat{i}", [P, TOK]) for i in range(4)]
        ma = [a.take(f"ma{i}", [P, 384]) for i in range(3)]
        mb = [a.take(f"mb{i}", [P, 384]) for i in range(3)]
        a = Region(NORM, RTOP)
        ug, uv = a.take("ug", [P, UW]), a.take("uv", [P, UW])
        cg = a.take("cg", [P, TOK])
        a = Region(a.p, RTOP)
        cv = a.take("cv", [P, TOK])
        fr = a.take("fr", [20, 2, P])
        fw = [a.take(f"fw{i}", [P, 2, 20]) for i in range(2)]
        fso = a.take("fso", [P, 2, 18])
        fsot = a.take("fsot", [18, 2, P])
        a = Region(NORM + 2 * TOK * 4, RTOP)
        pl, ph = a.take("pl", [P, 2, TOK], F32R), a.take("ph", [P, 2, TOK], F32R)

        def f(t):
            return t.bitcast(F32)

        banks = [nc.alloc_psum_tensor(f"bank{i}", [P, 512], F32) for i in range(8)]
        ub = banks[0:3]

        def unit_bank(u):
            return banks[(u - WIDE0) % 6] if WIDE0 <= u < WIDE1 else ub[u % 3]

        sb_ = banks[3:5]
        pb_ = banks[5]
        mb_ = banks[6:8]

        x_in = [sem(f"x_in{g}") for g in range(NG)]
        const_in = sem("const_in")
        page_in = sem("page_in")
        raw_in = [sem("raw_in0"), sem("raw_in1")]
        pk_in = [sem("pk_in0"), sem("pk_in1")]
        pv_in = sem("pv_in")
        cwr_in = sem("cwr_in")
        gat_in = [sem("gat_in0"), sem("gat_in1")]
        x2_in = sem("x2_in")
        p_in = sem("p_in")
        stg_out = [sem(f"stg_out{g}") for g in range(NG)]
        vn_out = sem("vn_out")
        so_out = sem("so_out")
        y_out = [sem("y_out0"), sem("y_out1")]
        g_const = sem("g_const")
        g_fold = sem("g_fold")
        g_ss = sem("g_ss")
        g_self = sem("g_self")
        g_xl = sem("g_xl")
        g_acc0 = sem("g_acc0")
        g_lo = sem("g_lo")
        g_x = sem("g_x")
        a_hi = sem("a_hi")
        a_sq = sem("a_sq")
        a_m = sem("a_m")
        a_abs, a_exp, a_ln, a_lhi, a_a = (sem(n) for n in ("a_abs", "a_exp", "a_ln", "a_lhi", "a_a"))
        a_rt = sem("a_rt")
        a_self = sem("a_self")
        a_xhi = sem("a_xhi")
        a_sig = sem("a_sig")
        a_gelu = sem("a_gelu")
        a_nat = sem("a_nat")
        d_const = sem("d_const")
        d_lo = sem("d_lo")
        d_unit = sem("d_unit")
        d_r = sem("d_r")
        d_ms = sem("d_ms")
        d_self = sem("d_self")
        d_qbd = sem("d_qbd")
        d_z, d_sp, d_llo, d_sub = (sem(n) for n in ("d_z", "d_sp", "d_llo", "d_sub"))
        d_so = sem("d_so")
        d_t = sem("d_t")
        d_x = sem("d_x")
        d_xlo = sem("d_xlo")
        d_mrg = sem("d_mrg")
        d_cg = sem("d_cg")
        d_act = sem("d_act")
        d_e = sem("d_e")
        sp_held, pe_held = sem("sp_held"), sem("pe_held")
        p_unit = sem("p_unit")
        p_m = sem("p_m")
        p_sum = sem("p_sum")
        p_s, p_tri, p_comp, p_av = (sem(n) for n in ("p_s", "p_tri", "p_comp", "p_av"))

        xp = inp["x_prompt"].rearrange("n (b p) d -> p (n b) d", p=P)
        xsm = inp["x_sample"].rearrange("b t d -> (b t) d")
        ck = inp["cache_k"].rearrange("l n p h d -> (l n) p (h d)")
        cvv = inp["cache_v"].rearrange("l n p h d -> (l n) p (h d)")
        NPOOL = ck.shape[0]
        w_in = inp["w_in"].rearrange("l (k p) n -> p (l k) n", p=P)
        w_a = inp["w_a"].rearrange("l (k p) n -> p (l k) n", p=P)
        w_b = inp["w_b"].rearrange("l (k p) n -> p (l k) n", p=P)
        w_o = inp["w_o"].rearrange("l (k p) n -> p (l k) n", p=P)
        w_up = inp["w_up"].rearrange("l (k p) n -> p (l k) n", p=P)
        w_down = inp["w_down"].rearrange("l (k p) n -> p (l k) n", p=P)
        w_ple = inp["w_ple"].rearrange("l (k p) n -> p (l k) n", p=P)
        w_gate = inp["w_ple_gate"].rearrange("l (k p) n -> p (l k) n", p=P)
        pp = inp["p_prompt"].rearrange("l n (b p) d -> p (l n b) d", p=P)
        psm = inp["p_sample"].rearrange("l b t d -> (l b t) d")
        st_c = inp["state_conv"].rearrange("l b t c -> (l b t) c")
        st_f = inp["state_ffn_conv"].rearrange("l b t c -> (l b t) c")
        wc = inp["w_conv_a"].rearrange("l t c -> (l t) c")
        wf = inp["w_conv_f"].rearrange("l t c -> (l t) c")
        yp_o = out["y_prompt"].rearrange("n (b p) d -> p (n b) d", p=P)
        ys_o = out["y_sample"].rearrange("b t d -> (b t) d")
        kp_o, vp_o = (out[n].rearrange("l n (b p) h d -> p (l n b) (h d)", p=P) for n in ("k_prompt", "v_prompt"))
        ks_o, vs_o = (out[n].rearrange("l b t h d -> (l b t) (h d)") for n in ("k_sample", "v_sample"))
        cp_o = out["conv_prompt"].rearrange("l n t c -> (l n t) c")
        cs_o = out["conv_sample"].rearrange("l b t c -> (l b t) c")
        fp_o = out["ffn_conv_prompt"].rearrange("l n t c -> (l n t) c")
        fs_o = out["ffn_conv_sample"].rearrange("l b t c -> (l b t) c")

        IN_COLS = [(3 * CW, P), (4 * CW, P), (5 * CW, P), (CW, P), (2 * CW, P), (0, P),
                   (6 * CW, 2 * P), (6 * CW + P, 2 * P), (6 * CW + D, 2 * P), (6 * CW + D + P, 2 * P)]
        NIN = len(IN_COLS)
        NJOBS = NIN * NC4 + 8 + 8 + 4 + 60 + 2 + 2 + 8

        def block_rows(b):
            return P if b < BLK else NS

        def group_blocks(g):
            return range(3 * g, 3 * g + 3)

        def part(t, g):
            o, w = GROUPS[g]
            return t[..., o:o + w]

        def padded(t, g):
            o, w = GROUPS[g]
            if g < 2:
                return [(t[:, 2 + o:2 + o + w], slice(0, w))]
            return [(t[:, 2 + o:2 + SEQ], slice(0, SEQ - o)),
                    (t[:, US:UW].rearrange("p (b t) -> p b t", t=NT + 2)[:, :, 2:], slice(SEQ - o, w))]

        def like(ap, ref):
            return ap.rearrange("p (b t) -> p b t", t=NT) if len(ref.shape) == 3 else ap

        block = ctx.enter_context(nc.Block())

        @block.sync
        def _(sp):
            def hold(sem_, value):
                sp.wait_ge(sem_, value)
                sp.sem_inc(sp_held, 1)

            job = Count()

            def load(parts):
                if job.base >= 2:
                    hold(d_lo, job.at(-1))
                s = job.base % 2
                for dst, src in parts(raw[s]):
                    sp.dma_start(dst, src).then_inc(raw_in[s], 16)
                job.step()

            def tall(w, col):
                def parts(r):
                    r = r[:, :].rearrange("p (k n) -> p k n", n=P)
                    return [(r[:, 4 * i:4 * i + 4, :], w[:, 4 * i:4 * i + 4, ds(col, P)]) for i in range(2)]
                return parts

            def wide(w, k, col):
                def parts(r):
                    r = r[:, :].rearrange("p (k n) -> p k n", n=512)
                    return [(r[:, i:i + 1, :], w[:, ds(k + i, 1), col:col + 512]) for i in range(2)]
                return parts

            def in_job(c, n):
                start, stride = IN_COLS[n]
                return tall(w_in, c * stride + start)

            for g in range(NG):
                bs = [b for b in group_blocks(g) if b < BLK]
                sp.dma_start(xn[:, bs[0]:bs[-1] + 1, :], xp[:, bs[0]:bs[-1] + 1, :]).then_inc(x_in[g], 16)
                if g == NG - 1:
                    sp.dma_start(xn[0:NS, BLK, :], xsm).then_inc(x_in[g], 16)
                if g == 0:
                    for i, n in enumerate(GAINS):
                        sp.dma_start(gnat[i * KD:(i + 1) * KD, :], inp[n].rearrange("l (k p) -> (l k) p", p=P)).then_inc(const_in, 16)
                    sp.dma_start(brow[:, :], inp["sb_bias"]).then_inc(const_in, 16)
                    load(in_job(0, 0))
            load(in_job(0, 1))
            sp.dma_start(pgt[:, :], inp["page_table"].rearrange("b g -> (b g)").rearrange("(o n) -> o n", o=1)).then_inc(page_in, 16)
            hold(page_in, 16)

            miscn = Count()
            miscn.base = 2

            def rows_in(c):
                sp.dma_start(cwr[0:2 * NB, :], st_c[:, ds(c * P, P)]).then_inc(cwr_in, 16)
                sp.dma_start(cwr[2 * NB:2 * NB + 3, :], wc[:, ds(c * P, P)]).then_inc(cwr_in, 16)

            def cached(c, q, dst, src, done):
                for i in range(4):
                    e = 4 * q + i
                    pg, b = 1 - e // NB, e % NB
                    page = sp.value_load(pgt[0:1, b * PAGES + pg:b * PAGES + pg + 1], min_val=0, max_val=NPOOL - 1)
                    sp.dma_start(dst(q, i), src[ds(page, 1), :, ds(c * P, P)].rearrange("o p d -> p (o d)")).then_inc(done, 16)

            def keys(c, q):
                cached(c, q, lambda q, i: pk[:, q % 2, i, :], ck, pk_in[q % 2])

            def values(c, q):
                cached(c, q, lambda q, i: pv[:, 4 * q + i, :], cvv, pv_in)

            def gate_out(c, n, back=0):
                half, sub = (n - 6) // 2, (n - 6) % 2
                for g in range(NG):
                    o, w = GROUPS[g]
                    hold(d_unit, unitn.at(3 * n + g + 1 - back))
                    sp.dma_start(gate_spill[ds(half * KD + sub + 2 * c, 1), :, o:o + w].rearrange("o p t -> p (o t)"),
                                 stg[g][:, 0:w]).then_inc(stg_out[g], 16)

            unitn = Count()
            unitn.base = KD * NG

            def pair(c, last):
                load(in_job(c, 2))
                hold(p_m, miscn.at(2))
                keys(c, 2)
                load(in_job(c, 3))
                hold(p_m, miscn.at(3))
                keys(c, 3)
                for n in range(4, NIN):
                    load(in_job(c, n))
                    if n >= 8:
                        gate_out(c, n - 2)
                    if 4 <= n < 8:
                        values(c, n - 4)
                    if n == 7 and not last:
                        hold(p_m, miscn.at(11))
                        rows_in(c + 1)
                        keys(c + 1, 0)
                        keys(c + 1, 1)
                if not last:
                    load(in_job(c + 1, 0))
                    gate_out(c, NIN - 2)
                    load(in_job(c + 1, 1))
                    gate_out(c, NIN - 1)
                miscn.step(PM_ITER)
                unitn.step(3 * NIN)

            rows_in(0)
            keys(0, 0)
            keys(0, 1)
            with loop(sp, NC4 - 1, {job: NIN, miscn: PM_ITER, unitn: 3 * NIN}) as c:
                pair(c, False)
            pair(NC4 - 1, True)

            def ab_job(m):
                def parts(r):
                    r = r[:, :].rearrange("p (k n) -> p k n", n=P)
                    return [(r[:, 0:4, :], w_a[:, :, ds(m * P, P)]), (r[:, 4:8, :], w_b[:, :, ds(m * P, P)])]
                return parts

            load(ab_job(0))
            gate_out(NC4 - 1, NIN - 2, 3 * NIN)
            load(ab_job(1))
            gate_out(NC4 - 1, NIN - 1, 3 * NIN)
            per_g = [NC4 * 5, NC4 * 5, NC4 * 6]
            for g in range(NG):
                hold(stg_out[g], 16 * (1 + per_g[g]))
            hold(d_unit, unitn.at())
            hold(vn_out, 16 * NC4 * 4)
            hold(so_out, 16 * NC4 * 2)
            hold(a_m, 2 + NC4 * M_ITER)

            mrg = Count()

            def gates(m, s):
                for h in range(2):
                    sp.dma_start(gat[2 * s + h][:, :], gate_spill[ds(h * KD + m, 1), :, :].rearrange("o p t -> p (o t)")).then_inc(gat_in[s], 16)

            gates(0, 0)
            gates(1, 1)
            with loop(sp, 3, {job: 2, mrg: 2 * NG}) as t:
                for s in range(2):
                    load(ab_job(t * 2 + 2 + s))
                    mrg.step(NG)
                    hold(d_mrg, mrg.at())
                    gates(t * 2 + 2 + s, s)
            load(tall(w_o, 0))
            load(tall(w_o, P))
            hold(p_unit, ENDS[47])
            hold(d_mrg, 8 * NG)
            sp.dma_start(xn2[:, :, :], xp).then_inc(x2_in, 16)
            sp.dma_start(xn2s[:, :], xsm).then_inc(x2_in, 16)
            with loop(sp, 3, {job: 2}) as t:
                for s in range(2):
                    load(tall(w_o, (t * 2 + 2 + s) * P))

            def up_rows(t, misc):
                if misc is not None:
                    hold(p_m, misc)
                for h in range(2):
                    col = ds(t * P + h * FF, P)
                    sp.dma_start(fr[0:16, h, :], st_f[:, col]).then_inc(cwr_in, 16)
                    sp.dma_start(fr[16:19, h, :], wf[:, col]).then_inc(cwr_in, 16)
                    sp.dma_start(fr[19:20, h, :], inp["b_conv_f"][:, col]).then_inc(cwr_in, 16)

            mf = Count()
            mf.base = 2 + NC4 * PM_ITER
            up_rows(0, None)
            load(tall(w_up, 0))
            load(tall(w_up, FF))
            load(tall(w_up, P))
            load(tall(w_up, P + FF))
            up_rows(1, mf.at(1))

            def ffn(t):
                load(tall(w_up, (2 * t) * P))
                load(tall(w_up, (2 * t) * P + FF))
                up_rows(2 * t, mf.at(2))
                load(wide(w_down, 2 * t - 2, 0))
                load(wide(w_down, 2 * t - 2, 512))
                load(tall(w_up, (2 * t + 1) * P))
                load(tall(w_up, (2 * t + 1) * P + FF))
                up_rows(2 * t + 1, mf.at(4))
                mf.step(4)

            with loop(sp, 10, {job: 6, mf: 4}) as t:
                ffn(t + 1)
            sp.dma_start(pn[:, 0:BLK, :], pp).then_inc(p_in, 16)
            sp.dma_start(pn[0:NS, BLK, :], psm).then_inc(p_in, 16)
            load(wide(w_down, 20, 0))
            load(wide(w_down, 20, 512))
            load(wide(w_ple, 0, 0))
            load(wide(w_ple, 0, 512))
            load(tall(w_gate, 0))
            load(tall(w_gate, P))
            with loop(sp, 3, {job: 2}) as t:
                for s in range(2):
                    load(tall(w_gate, (t * 2 + 2 + s) * P))
            assert job.base == NJOBS, job.base
            hold(y_out[0], 16 * 5)
            hold(y_out[1], 16)
            hold(so_out, 16 * (NC4 * 2 + 22 * 4))

        @block.gpsimd
        def _(pool):
            me = Count()

            def then(ins):
                ins.then_inc(g_self, 1)
                pool.wait_ge(g_self, me.step())

            g = nc.gpsimd
            then(g.memset(ident[:, :], 0.0))
            g.affine_select(out=ident[:, :], in_=ident[:, :], compare_op=ALU.not_equal, fill=1.0, base=0,
                            pattern=[[-1, P]], channel_multiplier=1).then_inc(g_const, 1)
            then(g.memset(ones[:, :], 1.0))
            g.affine_select(out=trif[:, :], in_=ones[:, :], compare_op=ALU.is_ge, fill=0.0, base=0,
                            pattern=[[-1, P]], channel_multiplier=1)
            g.affine_select(out=compf[:, :], in_=ones[:, :], compare_op=ALU.is_gt, fill=0.0, base=0,
                            pattern=[[1, P]], channel_multiplier=-1)
            then(g.memset(far[:, :], 0.0))
            g.affine_select(out=far[:, :], in_=far[:, :], compare_op=ALU.is_gt, fill=FAR, base=0,
                            pattern=[[1, P]], channel_multiplier=-1)
            then(g.memset(fars[:, :], 0.0))
            new = fars[:, 0:P].rearrange("p (b h q) -> p b h q", b=NB, h=2)
            then(g.affine_select(out=new, in_=new, compare_op=ALU.is_gt, fill=FAR, base=0,
                                 pattern=[[NT, NB], [0, 2], [1, NT]], channel_multiplier=-1))
            g.affine_select(out=new, in_=new, compare_op=ALU.is_ge, fill=FAR, base=0,
                            pattern=[[-NT, NB], [0, 2], [0, NT]], channel_multiplier=1)
            g.memset(qbd[:, :, :, :], 0.0).then_inc(g_const, 1)

            job = Count()
            rawn = [Count(), Count()]
            sqn = Count()

            def fold(gain):
                s = job.base % 2
                pool.wait_ge(raw_in[s], rawn[s].step(32))
                if gain is None:
                    pool.wait_ge(g_fold, job.at())
                    pool.sem_inc(g_fold, 1)
                else:
                    r = raw[s][:, :].rearrange("p (k n) -> p k n", n=P)
                    gv = gains[:, gain * KD:(gain + 1) * KD].unsqueeze(2).to_broadcast([P, KD, P])
                    g.tensor_tensor(r, r, gv, ALU.mult).then_inc(g_fold, 1)
                job.step()

            def add_square(gr):
                k = sqn.base
                if k:
                    pool.wait_ge(g_ss, gsn.at())
                gsn.step()
                pool.wait_ge(a_sq, sqn.step())
                w = GROUPS[gr][1]
                g.tensor_tensor(part(ss[:, :], gr), part(ss[:, :], gr), sq[k % 2][:, 0:w], ALU.add).then_inc(g_ss, 1)

            def clear_sums():
                then(g.memset(ss[:, :], 0.0))

            gsn = Count()
            for _ in range(2):
                g.memset(ss[:, :], 0.0).then_inc(g_ss, 1)
                pool.wait_ge(g_ss, gsn.step())
            pool.wait_ge(a_m, 1)
            fold(0)
            fold(0)
            sqn.step(KD * NG)
            with loop(pool, NC4 - 1, {job: NIN, rawn[0]: 16 * NIN, rawn[1]: 16 * NIN}):
                for n in range(NIN):
                    fold(0)
            for n in range(NIN - 2):
                fold(0)
            with loop(pool, 4, {job: 2, rawn[0]: 32, rawn[1]: 32}):
                fold(None)
                fold(None)
            fold(None)
            fold(None)
            pool.wait_ge(d_mrg, 8 * NG)
            clear_sums()
            with loop(pool, 3, {job: 2, rawn[0]: 32, rawn[1]: 32, sqn: 6, gsn: 6}):
                for s in range(2):
                    for gr in range(NG):
                        add_square(gr)
                    fold(None)
            for s in range(2):
                for gr in range(NG):
                    add_square(gr)
                fold(2)
            order = [(gr, k) for gr in range(NG) for k in range(KD)]
            xhn = Count()
            xhn.base = XHI1

            def low(gr, k):
                pool.wait_ge(a_xhi, xhn.step())
                g.tensor_tensor(part(bl[:, k, :], gr), part(y[:, k, :], gr), part(f(bh[:, k, :]), gr), ALU.subtract).then_inc(g_lo, 1)

            for gr, k in order:
                low(gr, k)
                sqn.step()
            pool.wait_ge(a_sq, sqn.at())
            pool.wait_ge(g_lo, KD * NG)
            g.memset(y[:, :, :], 0.0).then_inc(g_acc0, 1)
            pool.wait_ge(d_r, 2 * NG)
            clear_sums()
            fold(2)
            fold(2)
            with loop(pool, 10, {job: 6, rawn[0]: 96, rawn[1]: 96}):
                fold(2)
                fold(2)
                fold(None)
                fold(None)
                fold(2)
                fold(2)
            fold(None)
            fold(None)
            pool.wait_ge(p_unit, ENDS[LAST_UP])
            for k in range(KD // 2):
                g.tensor_tensor(xw[:, k, :], f(bl[:, k, :]), f(bh[:, k, :]), ALU.add).then_inc(g_x, 1)
            fold(None)
            for m in range(KD):
                for gr in range(NG):
                    add_square(gr)
                if m == 0:
                    fold(None)
            fold(4)
            xhn.base = XHI2
            for i, (gr, k) in enumerate(order):
                low(gr, k)
                sqn.step()
                if i == 6:
                    fold(4)
            pool.wait_ge(d_r, 4 * NG)
            clear_sums()
            with loop(pool, 3, {job: 2, rawn[0]: 32, rawn[1]: 32, sqn: 6, gsn: 6}):
                for s in range(2):
                    fold(4)
                    for gr in range(NG):
                        add_square(gr)
            for s in range(2):
                for gr in range(NG):
                    add_square(gr)
            pool.wait_ge(p_unit, ENDS[-1])
            for gr, k in order:
                g.tensor_tensor(part(xw[:, k, :], gr), part(f(bl[:, k, :]), gr), part(f(bh[:, k, :]), gr), ALU.add).then_inc(g_xl, 1)
            assert job.base == NJOBS, job.base

        @block.scalar
        def _(act):
            s_ = nc.scalar
            me = Count()
            job, unit, sqn, mis, rtn = Count(), Count(), Count(), Count(), Count()
            gsn, smn, msn = Count(), Count(), Count()
            gsn.base = 2
            xhn = Count()

            def then(ins):
                ins.then_inc(a_self, 1)
                act.wait_ge(a_self, me.step())

            fld = Count()

            def ends(j):
                if fld.turn is None:
                    return ENDS[j]
                n, per = turn_jobs
                return ENDS[j + n] - per + fld.turn

            def whi():
                s = job.base % 2
                act.wait_ge(g_fold, job.at(1))
                if job.base >= 2:
                    act.wait_ge(p_unit, ends(job.base - 2))
                s_.activation(wh[s][:, :], raw[s][:, :], ACT.Copy).then_inc(a_hi, 1)
                job.step()

            pmn = Count()

            def evac(ops, done=None):
                b = mb_[mis.base % 2]
                mis.step()
                if done is None:
                    act.wait_ge(p_m, pmn.step())
                else:
                    act.wait_ge(p_av, done)
                for i, (dst, src) in enumerate(ops(b)):
                    ins = s_.activation(dst, src, ACT.Copy)
                ins.then_inc(a_m, 1)

            def square(src, gr):
                k = sqn.base
                act.wait_ge(g_ss, gsn.at(-1))
                gsn.step()
                sqn.step()
                s_.activation(sq[k % 2][:, 0:GROUPS[gr][1]], src, ACT.Square).then_inc(a_sq, 1)

            def square_summed(src, gr, i):
                if i == 0:
                    act.wait_ge(g_ss, gsn.at())
                if i >= 2:
                    act.wait_ge(p_sum, smn.at(i - 1))
                k = sqn.base
                sqn.step()
                s_.activation(sq[k % 2][:, 0:GROUPS[gr][1]], src, ACT.Square).then_inc(a_sq, 1)

            def rsqrt(summed=False):
                for gr in range(NG):
                    if summed:
                        act.wait_ge(d_ms, msn.step())
                    else:
                        act.wait_ge(d_unit, unit.step())
                    then(s_.activation(part(rt[:, :], gr), part(ms[:, :], gr), ACT.Ln))
                    s_.activation(part(rt[:, :], gr), part(rt[:, :], gr), ACT.Exp, scale=-0.5).then_inc(a_rt, 1)

            def tables(name):
                s_.preload_act_table_set(name)

            tables("natural_log_exp_and_others")
            for gr in range(NG):
                for k in range(KD):
                    act.wait_ge(p_unit, unit.step())
                    b = ub[(unit.base - 1) % 3][:, 0:GROUPS[gr][1]]
                    s_.activation(part(xh[:, k, :], gr), b, ACT.Copy)
                    square_summed(b, gr, gr * KD + k)
                if gr == 0:
                    evac(lambda b: [(gains[:, :], b[:, 0:6 * KD])])
                    evac(lambda b: [(bias[:, :], b[:, 0:8])])
                if gr == 1:
                    whi()
            smn.step(KD * NG)
            rsqrt(True)

            stn = [Count() for _ in range(NG)]
            for g in range(NG):
                act.sem_inc(stg_out[g], 16)
                stn[g].base = 16
            vno, soo, att = Count(), Count(), Count()

            def pair(c):
                evac(lambda b: [(cwt[:, :], b[:, 0:19])])
                whi()
                evac(lambda b: [(pkT[:, 0:512], b[:, :])])
                whi()
                for q in range(1, 4):
                    evac(lambda b: [(pkT[:, q * 512:(q + 1) * 512], b[:, :])])
                whi()
                def natural(kind, g):
                    if kind == 0:
                        act.wait_ge(stg_out[g], stn[g].at())
                        dst = stg[g][:, :].rearrange("p (b n) -> p b n", n=P)
                    else:
                        dst = vn[:, 3 * g:3 * g + 3, :]

                    def ops(b):
                        b = b[:, 0:384].rearrange("p (b n) -> p b n", n=P)
                        if g < 2:
                            return [(dst, b)]
                        return [(dst[:, 0:2, :], b[:, 0:2, :]), (dst[0:NS, 2, :], b[0:NS, 2, :])]
                    evac(ops)
                    act.wait_ge(a_m, mis.at())
                    o, os_, sm = (kp_o, ks_o, stg_out[g]) if kind == 0 else (vp_o, vs_o, vn_out)
                    nb = 3 if g < 2 else 2
                    act.dma_start(o[:, 3 * g:3 * g + nb, ds(c * P, P)], dst[:, 0:nb, :]).then_inc(sm, 16)
                    if g == 2:
                        act.dma_start(os_[:, ds(c * P, P)], dst[0:NS, 2, :]).then_inc(sm, 16)
                    if kind == 0:
                        stn[g].step(16 if g < 2 else 32)

                for g in range(NG):
                    natural(0, g)
                natural(1, 0)
                for g in range(NG):
                    stn[g].step(64)

                for n in range(SLOTS):
                    if n >= 1 and n - 1 < NSTEP:
                        s = n - 1
                        w = step_shape(s)[1]
                        act.wait_ge(d_sp, att.at(s + 1))
                        if s - 2 in COMPS:
                            act.wait_ge(p_comp, cmp.at(COMPS.index(s - 2) + 1))
                        elif s >= 2:
                            act.wait_ge(p_tri, att.at(s - 1))
                        s_.activation(lh[s % 2][:, 0:w], tt[s % 2][:, 0:w], ACT.Copy).then_inc(a_lhi, 1)
                    if n >= 2 and n - 2 < NSTEP:
                        s = n - 2
                        w = step_shape(s)[1]
                        act.wait_ge(d_sub, att.at(s + 1))
                        if s >= 2:
                            act.wait_ge(p_av, att.at(s - 1))
                        s_.activation(aa[s % 2][:, 0:w], z[s % 3][:, 0:w], ACT.Exp).then_inc(a_a, 1)
                    if n < NSTEP:
                        act.wait_ge(d_z, att.at(n + 1))
                        if n >= 2:
                            act.wait_ge(d_llo, att.at(n - 1))
                        w = step_shape(n)[1]
                        t = tt[n % 2][:, 0:w]
                        s_.activation(t, z[n % 3][:, 0:w], ACT.Abs).then_inc(a_abs, 1)
                        act.wait_ge(a_abs, att.at(n + 1))
                        s_.activation(t, t, ACT.Exp, scale=-1.0).then_inc(a_exp, 1)
                        act.wait_ge(a_exp, att.at(n + 1))
                        s_.activation(t, t, ACT.Ln, bias=1.0).then_inc(a_ln, 1)
                    if FILL_AT.get(n, 1) % 3 == 0:
                        whi()
                    if n < NG - 1:
                        natural(1, n + 1)
                    if n >= 3 and step_shape(n - 3)[4]:
                        s = n - 3
                        if s == SAMPLE:
                            def ops(b):
                                src = b[:, 0:P].rearrange("p (b h q) -> p b h q", b=NB, h=2)
                                r = []
                                for h in range(2):
                                    rows = slice(64 * h, 64 * h + 64)
                                    r.append((oT[rows, ds(c, 1), SEQ:TOK].rearrange("p o (b q) -> p (o b) q", q=NT), src[rows, :, h, :]))
                                return r
                        else:
                            h, qh, _ = STEPS[s]

                            def ops(b, h=h, qh=qh):
                                rows = slice(64 * h, 64 * h + 64)
                                return [(oT[rows, ds(c, 1), qh * 512:qh * 512 + 512].rearrange("p o t -> p (o t)"), b[rows, :])]
                        evac(ops, att.at(s + 1))
                vno.step(64)
                att.step(NSTEP)
                cmp.step(len(COMPS))
                fld.step(3 * NIN)
                evac(lambda b: [(sot[0:2, 0, :], b[0:2, 0:P])])
                act.wait_ge(a_m, mis.at())
                act.dma_start(cp_o[:, ds(c * P, P)], sot[0:2, 0, :]).then_inc(so_out, 16)
                evac(lambda b: [(sot[:, 1, :], b[0:2 * NB, 0:P])])
                act.wait_ge(a_m, mis.at())
                act.dma_start(cs_o[:, ds(c * P, P)], sot[:, 1, :]).then_inc(so_out, 16)
                soo.step(32)
                act.wait_ge(vn_out, vno.at())
                act.wait_ge(so_out, soo.at())

            cmp = Count()
            turn_jobs = (NIN, 3 * NIN)
            with loop(act, NC4, {fld: 3 * NIN, job: NIN, mis: M_ITER, pmn: PM_ITER, att: NSTEP, cmp: len(COMPS), stn[0]: 80, stn[1]: 80,
                                 stn[2]: 96, vno: 64, soo: 32}) as c:
                pair(c)
            unit.base += 3 * NIN * NC4

            act.wait_ge(p_unit, ENDS[39])
            act.wait_ge(d_unit, ENDS[39])
            for src, dst in ((cout, ch), (oT, oh)):
                for k in range(NC4):
                    s_.activation(dst[:, k, :], src[:, k, :], ACT.Copy).then_inc(a_xhi, 1)
                    xhn.step()

            gn = [Count(), Count()]
            mrg = Count()
            tables("sigmoid_and_others")

            def merge(s):
                act.wait_ge(gat_in[s], gn[s].step(32))
                for h in range(2):
                    s_.activation(gat[2 * s + h][:, :], gat[2 * s + h][:, :], ACT.Sigmoid).then_inc(a_sig, 1)

            def merge_hi(m):
                for gr in range(NG):
                    act.wait_ge(d_x, mrg.step())
                    s_.activation(part(bh[:, ds(m, 1), :].rearrange("p o t -> p (o t)"), gr), ma[gr][:, 0:GROUPS[gr][1]],
                                  ACT.Copy).then_inc(a_xhi, 1)
                    xhn.step()

            turn_jobs = (2, 12)
            with loop(act, 4, {fld: 12, job: 2, mrg: 6, xhn: 6, gn[0]: 32, gn[1]: 32}) as t:
                for s in range(2):
                    whi()
                    merge(s)
                    merge_hi(t * 2 + s)
                fld.step(12)
            unit.base += 48

            def squares(m):
                for gr in range(NG):
                    act.wait_ge(d_unit, unit.step())
                    square(part(y[:, ds(m, 1), :].rearrange("p o t -> p (o t)"), gr), gr)

            tables("natural_log_exp_and_others")
            act.wait_ge(p_sum, smn.at())
            act.wait_ge(d_mrg, 8 * NG)
            turn_jobs = (2, 6)
            with loop(act, 4, {fld: 6, job: 2, unit: 6, sqn: 6, gsn: 6}) as t:
                for s in range(2):
                    whi()
                    squares(t * 2 + s)
                fld.step(6)
            rsqrt()
            dxn = Count()
            dxn.base = 8 * NG

            def update(done, n):
                for gr in range(NG):
                    for k in range(KD):
                        act.wait_ge(done, n.step())
                        s_.activation(part(bh[:, k, :], gr), part(y[:, k, :], gr), ACT.Copy).then_inc(a_xhi, 1)
                        xhn.step()
                        square_summed(part(y[:, k, :], gr), gr, gr * KD + k)
                smn.step(24)

            update(d_unit, unit)
            rsqrt(True)

            cgn, acn = Count(), Count()

            def rows(pr):
                evac(lambda b: [(fw[pr][:, :, :], b[:, 0:40].rearrange("p (h n) -> p h n", h=2))])

            def gelu():
                act.wait_ge(d_cg, cgn.step())
                s_.activation(cg[:, :], cg[:, :], ACT.Gelu_apprx_tanh).then_inc(a_gelu, 1)

            def act_hi(k):
                act.wait_ge(d_act, acn.step())
                s_.activation(fh[:, k, :], cg[:, :], ACT.Copy).then_inc(a_xhi, 1)
                xhn.step()

            def states(t):
                act.wait_ge(so_out, soo.at())
                evac(lambda b: [(fsot[:, :, :], b[0:18, 0:2 * P].rearrange("r (h n) -> r h n", h=2))])
                act.wait_ge(a_m, mis.at())
                for h in range(2):
                    act.dma_start(fp_o[:, ds(t * P + h * FF, P)], fsot[0:2, h, :]).then_inc(so_out, 16)
                    act.dma_start(fs_o[:, ds(t * P + h * FF, P)], fsot[2:18, h, :]).then_inc(so_out, 16)
                soo.step(64)

            def ffn(t, first):
                rows(0)
                whi()
                if not first:
                    states(t * 2 - 1)
                whi()
                gelu()
                if not first:
                    whi()
                    whi()
                    act.wait_ge(p_unit, unit.at(30))
                act_hi(0)
                rows(1)
                whi()
                states(t * 2)
                whi()
                gelu()
                act_hi(1)
                unit.step(12 if first else 36)
                if not first:
                    fld.step(36)

            tables("gelu_apprx_tanh_and_others")
            ffn(0, True)
            turn_jobs = (6, 36)
            with loop(act, 10, {fld: 36, unit: 36, job: 6, mis: 4, pmn: 4, cgn: 2, acn: 2, soo: 128, xhn: 2}) as t:
                ffn(t + 1, False)
            states(NFF - 1)
            act.wait_ge(so_out, soo.at())
            tables("natural_log_exp_and_others")
            act.wait_ge(p_sum, smn.at())
            u0 = unit.base

            def squares_of(m):
                for gr in range(NG):
                    act.wait_ge(d_unit, u0 + NG * m + gr + 1)
                    square(part(y[:, m, :], gr), gr)

            whi()
            whi()
            for m in range(KD // 2):
                squares_of(m)
            unit.base += KD * NG
            for i in range(2 * NG):
                act.wait_ge(p_unit, unit.step())
                gr, k = i // 2, i % 2
                s_.activation(part(ph[:, k, :], gr), ub[(unit.base - 1) % 3][:, 0:GROUPS[gr][1]], ACT.Copy).then_inc(a_xhi, 1)
                xhn.step()
            whi()
            for m in range(KD // 2, KD):
                squares_of(m)
            unit.base += KD * NG // 2
            whi()
            rsqrt()
            unit.base += KD * NG // 2
            assert xhn.base == XHI2
            act.wait_ge(g_x, KD // 2)
            update(d_x, dxn)
            rsqrt(True)

            en, sg = Count(), Count()
            tables("sigmoid_and_others")

            def gate(m):
                for gr in range(NG):
                    act.wait_ge(d_unit, unit.step())
                    t = tmp[gr][:, 0:GROUPS[gr][1]]
                    s_.activation(t, t, ACT.Sigmoid).then_inc(a_sig, 1)
                    act.wait_ge(d_e, en.step())
                    square(part(y[:, ds(m, 1), :].rearrange("p o t -> p (o t)"), gr), gr)

            act.wait_ge(p_sum, smn.at())
            turn_jobs = (2, 6)
            with loop(act, 3, {fld: 6, job: 2, unit: 6, sqn: 6, gsn: 6, en: 6}) as t:
                for s in range(2):
                    whi()
                    gate(t * 2 + s)
                fld.step(6)
            whi()
            gate(6)
            gate(7)
            tables("natural_log_exp_and_others")
            rsqrt()
            assert job.base == NJOBS, job.base
            for i in range(NG * KD):
                gr, k = i // KD, i % KD
                if k == 0 and gr == 2:
                    act.wait_ge(y_out[0], 16)
                act.wait_ge(p_unit, unit.step())
                b = ub[(unit.base - 1) % 3][:, 0:384].rearrange("p (b n) -> p b n", n=P)
                o = on[:, gr % 2, :, k * P:(k + 1) * P]
                if gr < 2:
                    s_.activation(o, b, ACT.Copy).then_inc(a_nat, 1)
                else:
                    s_.activation(o[:, 0:2, :], b[:, 0:2, :], ACT.Copy)
                    s_.activation(o[0:NS, 2, :], b[0:NS, 2, :], ACT.Copy).then_inc(a_nat, 1)
                half = slice((k // 4) * 512, (k // 4) * 512 + 512)
                if k == KD - 1 and gr < 2:
                    act.wait_ge(a_nat, i + 1)
                    act.dma_start(yp_o[:, 3 * gr:3 * gr + 3, :], on[:, gr % 2, :, :]).then_inc(y_out[gr], 16)
                elif k % 4 == 3 and gr == 2:
                    act.wait_ge(a_nat, i + 1)
                    act.dma_start(yp_o[:, 3 * gr:BLK, half], on[:, 0, 0:2, half]).then_inc(y_out[0], 16)
                    act.dma_start(ys_o[:, half], on[0:NS, 0, 2, half]).then_inc(y_out[0], 16)

        @block.vector
        def _(dve):
            v = nc.vector
            me = Count()
            job, unit, rtn, xhn, msn = Count(), Count(), Count(), Count(), Count()

            def then(ins):
                ins.then_inc(d_self, 1)
                dve.wait_ge(d_self, me.step())

            def wlo():
                s = job.base % 2
                dve.wait_ge(a_hi, job.step())
                v.tensor_tensor(wl[s][:, :], raw[s][:, :], f(wh[s][:, :]), ALU.subtract).then_inc(d_lo, 1)

            def bank(gr):
                u = unit.base
                dve.wait_ge(p_unit, unit.step())
                return unit_bank(u)[:, 0:GROUPS[gr][1]]

            def mean(gr, summed=None):
                if summed is None:
                    v.tensor_scalar(part(ms[:, :], gr), bank(gr), 1.0 / D, EPS, ALU.mult, ALU.add).then_inc(d_unit, 1)
                else:
                    dve.wait_ge(p_sum, summed + KD * (gr + 1))
                    v.tensor_scalar(part(ms[:, :], gr), banks[3 + gr][:, 0:GROUPS[gr][1]], 1.0 / D, EPS, ALU.mult, ALU.add).then_inc(d_ms, 1)
                    msn.step()

            def newton(gr, summed=None):
                if summed is None:
                    dve.wait_ge(d_unit, unit.at())
                else:
                    dve.wait_ge(d_ms, msn.at())
                dve.wait_ge(a_rt, rtn.step())
                r0, m, r = (part(x[:, :], gr) for x in (rt, ms, rs))
                t = tmp[gr % 2][:, 0:GROUPS[gr][1]]
                then(v.tensor_tensor(t, r0, r0, ALU.mult))
                then(v.scalar_tensor_tensor(out=t, in0=t, scalar=-0.5, in1=m, op0=ALU.mult, op1=ALU.mult))
                v.scalar_tensor_tensor(out=r, in0=t, scalar=1.5, in1=r0, op0=ALU.add, op1=ALU.mult).then_inc(d_r, 1)

            def rstat(summed=None):
                for gr in range(NG):
                    mean(gr, summed)
                for gr in range(NG):
                    newton(gr, summed)
                dve.wait_ge(d_r, rtn.at())

            dve.wait_ge(g_const, 2)
            v.tensor_copy(tri[:, :], trif[:, :])
            v.tensor_copy(comp[:, :], compf[:, :])
            v.tensor_copy(full[:, :], ones[:, :]).then_inc(d_const, 1)
            for gr in range(NG):
                for k in range(KD):
                    b = bank(gr)
                    dve.wait_ge(a_sq, unit.at())
                    v.tensor_tensor(part(xl[:, k, :], gr), b, part(f(xh[:, k, :]), gr), ALU.subtract).then_inc(d_unit, 1)
            wlo()
            rstat(0)

            pm, mis, att, stn, son = Count(), Count(), Count(), [Count() for _ in range(NG)], Count()
            cmp = Count()

            def scaled(dst, b, gr):
                v.tensor_tensor(dst, b, part(rs[:, :], gr), ALU.mult).then_inc(d_unit, 1)

            def conv(src, dsts, w, bcol, done):
                views = [(lambda j: src[:, j:j + SEQ], dsts[0]),
                         (lambda j: src[:, US:UW].rearrange("p (b t) -> p b t", t=NT + 2)[:, :, j:j + NT], dsts[1])]
                for j in range(3):
                    for i, (xv, d) in enumerate(views):
                        if j == 0 and bcol is None:
                            ins = v.tensor_scalar(d, xv(0), w[0], None, ALU.mult)
                        elif j == 0:
                            ins = v.tensor_scalar(d, xv(0), w[0], bcol, ALU.mult, ALU.add)
                        else:
                            ins = v.scalar_tensor_tensor(out=d, in0=xv(j), scalar=w[j], in1=d, op0=ALU.mult, op1=ALU.add)
                        if j == 2 and i == 1 and done is not None:
                            ins.then_inc(done, 1)
                        elif i == 1:
                            then(ins)
                        yield

            def split_cols(t):
                return t[:, 0:SEQ], t[:, SEQ:TOK].rearrange("p (b t) -> p b t", t=NT)

            def pair(c):
                v.tensor_copy(bias2[:, 0:2], bias[:, ds(c * 2, 2)])
                then(v.tensor_scalar(bias2[:, 2:4], bias[:, ds(c * 2, 2)], 1 / SCALE, None, ALU.mult))
                mv = fars[:, :].rearrange("p (n h q) -> p n h q", h=2, q=NT)
                bv = bfars[:, :].rearrange("p (n h q) -> p n h q", h=2, q=NT)
                for h in range(2):
                    then(v.tensor_scalar(bv[:, :, h, :], mv[:, :, h, :], bias2[:, 2 + h:3 + h], None, ALU.add))
                wlo()
                for gr in range(NG):
                    scaled(part(qT[:, :], gr), bank(gr), gr)
                dve.wait_ge(d_unit, unit.at())
                for h in range(2):
                    rows = slice(64 * h, 64 * h + 64)
                    ins = v.tensor_copy(qbd[rows, :, h, :], qT[rows, SEQ:TOK].rearrange("p (b q) -> p b q", q=NT))
                ins.then_inc(d_qbd, 1)
                wlo()
                for gr in range(NG):
                    scaled(part(kT[:, :], gr), bank(gr), gr)
                wlo()
                dve.wait_ge(p_m, pm.at(5))
                for gr in range(NG):
                    scaled(part(vT[:, :], gr), bank(gr), gr)
                v.memset(uc[:, 0:2], 0.0)
                us = uc[:, US:UW].rearrange("p (b t) -> p b t", t=NT + 2)
                dve.wait_ge(a_m, mis.at(1))
                v.tensor_copy(us[:, :, 0:2], cwt[:, 0:16].rearrange("p (b t) -> p b t", t=2))

                taps = []

                def fill(i):
                    kind, gr = i // 3, i % 3
                    w = GROUPS[gr][1]
                    if kind == 2:
                        for _ in taps.pop() if taps else ():
                            pass
                    b = bank(gr)
                    if kind == 0:
                        for j, (d, cols) in enumerate(padded(uc, gr)):
                            ins = v.tensor_tensor(d, like(b[:, cols], d), like(part(rs[:, :], gr)[:, cols], d), ALU.mult)
                        ins.then_inc(d_unit, 1)
                    elif kind == 1:
                        scaled(tm1[:, 0:w], b, gr)
                        dve.wait_ge(d_unit, unit.at())
                        for d, cols in padded(uc, gr):
                            then(v.tensor_tensor(d, like(tm1[:, 0:w][:, cols], d), d, ALU.mult))
                        if gr == 2:
                            cc = cout[:, ds(c, 1), :].rearrange("p o t -> p (o t)")
                            wts = [cwt[:, 16 + j:17 + j] for j in range(3)]
                            dve.wait_ge(p_m, pm.at(0))
                            v.tensor_copy(so[:, 0:2], uc[:, SEQ:SEQ + 2])
                            v.tensor_copy(so[:, 2:18].rearrange("p (b t) -> p b t", t=2), us[:, :, NT:NT + 2]).then_inc(d_so, 1)
                            taps.append(conv(uc, split_cols(cc), wts, None, None))
                    elif kind == 2:
                        scaled(tm1[:, 0:w], b, gr)
                        dve.wait_ge(d_unit, unit.at())
                        cc = part(cout[:, ds(c, 1), :].rearrange("p o t -> p (o t)"), gr)
                        then(v.tensor_tensor(cc, cc, tm1[:, 0:w], ALU.mult))
                    else:
                        dve.wait_ge(stg_out[gr], stn[gr].at((16 if gr < 2 else 32) + 16 * (kind - 3)))
                        scaled(stg[gr][:, 0:w], b, gr)

                for n in range(SLOTS):
                    if n >= 1 and n - 1 < NSTEP:
                        s = n - 1
                        w = step_shape(s)[1]
                        dve.wait_ge(a_ln, att.at(s + 1))
                        t = tt[s % 2][:, 0:w]
                        v.scalar_tensor_tensor(out=t, in0=z[s % 3][:, 0:w], scalar=0.0, in1=t, op0=ALU.max, op1=ALU.add).then_inc(d_sp, 1)
                    if n >= 2 and n - 2 < NSTEP:
                        s = n - 2
                        o, w = step_shape(s)[:2]
                        dve.wait_ge(p_tri, att.at(s + 1))
                        v.tensor_tensor(z[s % 3][:, 0:w], z[s % 3][:, 0:w], pb_[:, o:o + w], ALU.subtract).then_inc(d_sub, 1)
                    if n < NSTEP:
                        w = step_shape(n)[1]
                        dve.wait_ge(p_s, att.at(n + 1))
                        if n >= 3:
                            dve.wait_ge(a_a, att.at(n - 2))
                        off = bias2[:, STEPS[n][0]:STEPS[n][0] + 1] if n < SAMPLE else 0.0
                        v.tensor_scalar(z[n % 3][:, 0:w], sb_[n % 2][:, 0:w], SCALE, off, ALU.mult, ALU.add).then_inc(d_z, 1)
                    i = FILL_AT.get(n)
                    if n >= 1 and n - 1 < NSTEP:
                        s = n - 1
                        w = step_shape(s)[1]
                        dve.wait_ge(a_lhi, att.at(s + 1))
                        v.tensor_tensor(ll[s % 2][:, 0:w], tt[s % 2][:, 0:w], f(lh[s % 2][:, 0:w]), ALU.subtract).then_inc(d_llo, 1)
                    if i is not None:
                        fill(i)
                        if i % 3 == 0:
                            wlo()
                    for op in taps:
                        next(op, None)
                        next(op, None)
                att.step(NSTEP)
                mis.step(M_ITER)
                pm.step(PM_ITER)
                for gr in range(NG):
                    stn[gr].step(80 if gr < 2 else 96)

            mis.base = pm.base = 2
            for g in range(NG):
                stn[g].base = 16
            with loop(dve, NC4, {job: NIN, unit: 3 * NIN, mis: M_ITER, pm: PM_ITER, att: NSTEP, stn[0]: 80, stn[1]: 80,
                                 stn[2]: 96, me: PAIR_SELF}) as c:
                pair(c)

            dve.wait_ge(d_self, me.at())
            for src, hi, lo in ((cout, ch, cl), (oT, oh, ol)):
                for k in range(NC4):
                    dve.wait_ge(a_xhi, xhn.step())
                    v.tensor_tensor(lo[:, k, :], src[:, k, :], f(hi[:, k, :]), ALU.subtract).then_inc(d_xlo, 1)

            sg, mg = Count(), Count()

            def merge(m, s):
                dve.wait_ge(a_sig, sg.at(1))
                for gr in range(NG):
                    b = bank(gr)
                    v.tensor_tensor(ma[gr][:, 0:GROUPS[gr][1]], b, part(gat[2 * s][:, :], gr), ALU.mult).then_inc(d_unit, 1)
                dve.wait_ge(a_sig, sg.at(2))
                sg.step(2)
                for gr in range(NG):
                    w = GROUPS[gr][1]
                    b = bank(gr)
                    v.tensor_tensor(mb[gr][:, 0:w], b, part(gat[2 * s + 1][:, :], gr), ALU.mult).then_inc(d_unit, 1)
                    dve.wait_ge(d_unit, unit.at())
                    v.tensor_tensor(ma[gr][:, 0:w], ma[gr][:, 0:w], mb[gr][:, 0:w], ALU.add).then_inc(d_x, 1)
                for gr in range(NG):
                    dve.wait_ge(a_xhi, xhn.step())
                    hi = part(bh[:, ds(m, 1), :].rearrange("p o t -> p (o t)"), gr)
                    lo = part(bl[:, ds(m, 1), :].rearrange("p o t -> p (o t)"), gr)
                    v.tensor_tensor(lo, ma[gr][:, 0:GROUPS[gr][1]], f(hi), ALU.subtract).then_inc(d_mrg, 1)
                dve.wait_ge(d_mrg, mg.step(NG))

            with loop(dve, 4, {job: 2, unit: 12, xhn: 6, sg: 4, mg: 6}) as t:
                for s in range(2):
                    wlo()
                    merge(t * 2 + s, s)

            def plain(m):
                for gr in range(NG):
                    b = bank(gr)
                    v.tensor_copy(part(y[:, ds(m, 1), :].rearrange("p o t -> p (o t)"), gr), b).then_inc(d_unit, 1)

            with loop(dve, 4, {job: 2, unit: 6}) as t:
                for s in range(2):
                    wlo()
                    plain(t * 2 + s)

            tn = Count()

            def normed(gain, gr, k):
                yy = part(y[:, k, :], gr)
                col = gain * KD + k
                v.scalar_tensor_tensor(out=yy, in0=yy, scalar=gains[:, col:col + 1], in1=part(rs[:, :], gr),
                                       op0=ALU.mult, op1=ALU.mult).then_inc(d_t, 1)
                tn.step()

            order = [(gr, k) for gr in range(NG) for k in range(KD)]

            def residual(gain, ready, add):
                for gr in range(NG):
                    mean(gr)
                for i in range(len(order) + 1):
                    if i < len(order):
                        gr, k = order[i]
                        if k == 0:
                            newton(gr)
                            dve.wait_ge(d_r, rtn.at())
                        normed(gain, gr, k)
                    if i:
                        ready(i)
                        add(*order[i - 1])
                    yield

            def last_normed(i):
                dve.wait_ge(d_t, tn.at(0 if i == len(order) else -1))

            def add_turned(gr, k):
                yy = part(y[:, k, :], gr)
                v.tensor_tensor(yy, yy, bank(gr), ALU.add).then_inc(d_unit, 1)

            for _ in residual(1, last_normed, add_turned):
                pass
            rstat(KD * NG)
            xhn.base += KD * NG

            mf = Count()
            mf.base = 2 + NC4 * M_ITER
            pmf = Count()
            pmf.base = 2 + NC4 * PM_ITER
            fln, gln, acn = Count(), Count(), Count()
            dve.wait_ge(g_acc0, 1)

            def states_in(pr, back):
                dve.wait_ge(a_m, mf.at(back))
                for h, u in enumerate((ug, uv)):
                    v.memset(u[:, 0:2], 0.0)
                    v.tensor_copy(u[:, US:UW].rearrange("p (b t) -> p b t", t=NT + 2)[:, :, 0:2],
                                  fw[pr][:, h, 0:16].rearrange("p (b t) -> p b t", t=2))

            def into(u):
                for gr in range(NG):
                    b = bank(gr)
                    for d, cols in padded(u, gr):
                        ins = v.tensor_tensor(d, like(b[:, cols], d), like(part(rs[:, :], gr)[:, cols], d), ALU.mult)
                    ins.then_inc(d_unit, 1)
                dve.wait_ge(d_unit, unit.at())

            def taps(pr, h):
                return [fw[pr][:, h, 16 + j:17 + j] for j in range(3)], fw[pr][:, h, 19:20]

            def conv_gate(pr):
                w, b = taps(pr, 0)
                return conv(ug, split_cols(cg), w, b, d_cg)

            def conv_val(pr):
                w, b = taps(pr, 1)
                yield from conv(uv, split_cols(cv), w, b, None)

            def states_out(back):
                dve.wait_ge(p_m, pmf.at(back))
                for h, u in enumerate((ug, uv)):
                    v.tensor_copy(fso[:, h, 0:2], u[:, SEQ:SEQ + 2])
                    ins = v.tensor_copy(fso[:, h, 2:18].rearrange("p (b t) -> p b t", t=2),
                                        u[:, US:UW].rearrange("p (b t) -> p b t", t=NT + 2)[:, :, NT:NT + 2])
                ins.then_inc(d_so, 1)

            def times():
                dve.wait_ge(a_gelu, gln.step())
                v.tensor_tensor(cg[:, :], cg[:, :], cv[:, :], ALU.mult).then_inc(d_act, 1)
                acn.step()

            def act_lo(k):
                dve.wait_ge(a_xhi, xhn.step())
                v.tensor_tensor(fl[:, k, :], cg[:, :], f(fh[:, k, :]), ALU.subtract).then_inc(d_xlo, 1)

            def down_unit(m, gr):
                b = bank(gr)
                yy = part(y[:, m, :], gr)
                v.tensor_tensor(yy, yy, b, ALU.add).then_inc(d_unit, 1)

            def ffn(first):
                wlo()
                states_in(0, 1)
                into(ug)
                wlo()
                for _ in conv_gate(0):
                    pass
                into(uv)
                states_out(0 if first else 2)
                cvg = conv_val(0)
                if not first:
                    for half in range(2):
                        wlo()
                        for i in range(12):
                            down_unit(4 * half + i // 3, i % 3)
                            if i % 4 == 3:
                                next(cvg)
                for _ in cvg:
                    pass
                times()
                act_lo(0)
                wlo()
                states_in(1, 2 if first else 3)
                into(ug)
                wlo()
                for _ in conv_gate(1):
                    pass
                into(uv)
                states_out(3 if first else 4)
                for _ in conv_val(1):
                    pass
                times()
                act_lo(1)
                mf.step(3 if first else 4)
                pmf.step(3 if first else 4)

            ffn(True)
            with loop(dve, 10, {job: 6, unit: 36, mf: 4, pmf: 4, gln: 2, acn: 2, xhn: 2, me: FFN_SELF}) as t:
                ffn(False)
            for half in range(2):
                wlo()
                for i in range(12):
                    down_unit(4 * half + i // 3, i % 3)
                    if i % 6 == 5:
                        k = KD // 2 + 2 * half + i // 6
                        v.tensor_tensor(xw[:, k, :], f(bl[:, k, :]), f(bh[:, k, :]), ALU.add)
            for i in range(6):
                gr, k = i // 2, i % 2
                b = bank(gr)
                dve.wait_ge(a_xhi, xhn.step())
                v.tensor_tensor(part(pl[:, k, :], gr), b, part(f(ph[:, k, :]), gr), ALU.subtract).then_inc(d_unit, 1)
            def add_whole(gr, k):
                yy = part(y[:, k, :], gr)
                v.tensor_tensor(yy, yy, part(xw[:, k, :], gr), ALU.add).then_inc(d_x, 1)

            dve.wait_ge(g_x, KD // 2)
            res = residual(3, last_normed, add_whole)
            for m in range(KD):
                if m % 4 == 0:
                    wlo()
                for gr in range(NG):
                    if m >= KD // 2:
                        next(res)
                    v.tensor_copy(part(ple[:, m, :], gr), bank(gr)).then_inc(d_unit, 1)
            for _ in res:
                pass
            rstat(2 * KD * NG)
            en, sgn = Count(), Count()
            sgn.base = 16

            def gate(m):
                for gr in range(NG):
                    w = GROUPS[gr][1]
                    scaled(tmp[gr][:, 0:w], bank(gr), gr)
                    dve.wait_ge(a_sig, sgn.step())
                    e = part(y[:, ds(m, 1), :].rearrange("p o t -> p (o t)"), gr)
                    v.tensor_tensor(e, tmp[gr][:, 0:w], part(ple[:, ds(m, 1), :].rearrange("p o t -> p (o t)"), gr),
                                    ALU.mult).then_inc(d_e, 1)

            with loop(dve, 3, {job: 2, unit: 6, sgn: 6}) as t:
                for s in range(2):
                    wlo()
                    gate(t * 2 + s)
            wlo()
            gate(6)
            gate(7)
            assert job.base == NJOBS, job.base

            def whole_too(i):
                last_normed(i)
                dve.wait_ge(g_xl, i)

            for _ in residual(5, whole_too, add_whole):
                pass

        @block.tensor
        def _(pe):
            t_ = nc.tensor
            job, unit, mis, att, cmp = Count(), Count(), Count(), Count(), Count()

            def free_bank():
                u = unit.base
                if WIDE0 <= u < WIDE0 + 6:
                    pe.wait_ge(d_unit, WIDE0)
                    if u == WIDE0 + 3:
                        pe.wait_ge(d_ms, 2 * NG)
                elif WIDE0 <= u < WIDE1:
                    pe.wait_ge(d_unit, unit.at(-5))
                elif WIDE1 <= u < WIDE1 + 3:
                    pe.wait_ge(d_unit, WIDE1)
                elif u >= 3:
                    pe.wait_ge(d_unit, unit.at(-2))
                unit.step()
                return unit_bank(u)

            def products(gr, terms, last_of_job=False):
                b = free_bank()[:, 0:GROUPS[gr][1]]
                n = len(terms)
                for i, (h, l, xhi, xlo) in enumerate(terms):
                    t_.matmul(b, h, xhi, start=(i == 0), stop=False)
                    t_.matmul(b, h, xlo, start=False, stop=False)
                    ins = t_.matmul(b, l, xhi, start=False, stop=(i == n - 1))
                ins.then_inc(p_unit, 1)
                return ins

            def begin_job():
                pe.wait_ge(d_lo, job.step())

            def tall(s, k):
                return wh[s][:, k * P:(k + 1) * P], wl[s][:, k * P:(k + 1) * P]

            def tile(gr, s, hi, lo, ks=range(KD), k0=0):
                products(gr, [(*tall(s, k), part(hi[:, k - k0, :], gr), part(lo[:, k - k0, :], gr)) for k in ks])

            def stat():
                for gr in range(NG):
                    b = free_bank()[:, 0:GROUPS[gr][1]]
                    pe.wait_ge(g_ss, ssn.base)
                    t_.matmul(b, ones[:, :], part(ss[:, :], gr), start=True, stop=True).then_inc(p_unit, 1)

            ssn, sqn = Count(), Count()
            ssn.base = 2

            def summed(i):
                gr, k = i // KD, i % KD
                j = sqn.base
                pe.wait_ge(a_sq, sqn.step())
                t_.matmul(banks[3 + gr][:, 0:GROUPS[gr][1]], ones[:, :], sq[j % 2][:, 0:GROUPS[gr][1]],
                          start=(k == 0), stop=(k == KD - 1), skip_group_check=True).then_inc(p_sum, 1)

            def misc():
                pe.wait_ge(a_m, mis.at(-1))
                b = mb_[mis.base % 2]
                mis.step()
                return b

            pe.wait_ge(g_const, 2)

            def turned(b, src, rows=P):
                return t_.transpose(b, src, ident[0:rows, 0:rows])

            def x_turned(gr, k, nat, smp):
                b = free_bank()
                for j, bl_ in enumerate(group_blocks(gr)):
                    if bl_ < BLK:
                        ins = turned(b[:, j * P:(j + 1) * P], nat[:, bl_, k * P:(k + 1) * P])
                    else:
                        ins = turned(b[:, j * P:j * P + NS], smp[:, k * P:(k + 1) * P], NS)
                ins.then_inc(p_unit, 1)

            for i in range(NG * KD + 2):
                gr, k = i // KD, i % KD
                if i < NG * KD:
                    if k == 0:
                        pe.wait_ge(x_in[gr], 32 if gr == 2 else 16)
                    x_turned(gr, k, xn, xn[0:NS, BLK, :])
                if i >= 2:
                    summed(i - 2)
                if i == KD:
                    pe.wait_ge(const_in, 16 * 7)
                    t_.transpose(mb_[0][:, 0:6 * KD], gnat[:, :], ident[0:6 * KD, 0:6 * KD]).then_inc(p_m, 1)
                    t_.matmul(mb_[1][:, 0:8], ones[0:1, :], brow[:, :], start=True, stop=True).then_inc(p_m, 1)
                    mis.base = 2
            pe.wait_ge(d_const, 1)

            cwn, pkn, pvn, son, qn = Count(), [Count(), Count()], Count(), Count(), Count()

            def pair():
                u0 = unit.base
                b = misc()
                pe.wait_ge(cwr_in, cwn.step(32))
                pe.sem_inc(pe_held, 1)
                turned(b[:, 0:19], cwr[:, :], 19).then_inc(p_m, 1)

                def past(q):
                    b = misc()
                    pe.wait_ge(pk_in[q % 2], pkn[q % 2].step(64))
                    for i in range(4):
                        ins = turned(b[:, i * P:(i + 1) * P], pk[:, q % 2, i, :])
                    ins.then_inc(p_m, 1)

                def new_rows(src, u, gr):
                    pe.wait_ge(d_unit, unit.at(u + gr + 1 - (unit.base - u0)))
                    b = misc()
                    for j, bl_ in enumerate(group_blocks(gr)):
                        w = block_rows(bl_)
                        ins = turned(b[0:w, j * P:(j + 1) * P], src[:, bl_ * P:bl_ * P + w])
                    ins.then_inc(p_m, 1)

                begin_job()
                for gr in range(NG):
                    tile(gr, (job.base - 1) % 2, xh, xl)
                past(0)
                begin_job()
                for gr in range(NG):
                    tile(gr, (job.base - 1) % 2, xh, xl)
                    past(gr + 1)
                begin_job()
                for gr in range(NG):
                    tile(gr, (job.base - 1) % 2, xh, xl)
                    new_rows(kT, 3, gr)
                new_rows(vT, 6, 0)

                obank = {}

                def scores(s):
                    o, w, dg, first, last = step_shape(s)
                    b = sb_[s % 2]
                    if s >= 2:
                        pe.wait_ge(d_z, att.at(s - 1))
                    if s < SAMPLE:
                        h, qh, kb = STEPS[s]
                        rows = slice(64 * h, 64 * h + 64)
                        q0 = qh * 512 + o
                        ins = t_.matmul(b[:, 0:w], kT[rows, kb * P:(kb + 1) * P], qT[rows, q0:q0 + w], start=True, stop=True)
                        if dg:
                            ins = t_.matmul(b[:, 0:P], ident[:, :], far[:, :], start=False, stop=True, skip_group_check=True)
                    else:
                        pe.wait_ge(d_qbd, qn.step())
                        flat = qbd[:, :, :, :].rearrange("p b h q -> p (b h q)")
                        t_.matmul(b[:, 0:384], ident[:, :], bfars[:, :], start=True, stop=True, skip_group_check=True)
                        t_.matmul(b[0:NS, 0:P], kT[:, SEQ:TOK], flat, start=False, stop=True, skip_group_check=True)
                        for e in range(PAGES * NB):
                            ins = t_.matmul(b[:, P + 16 * e:P + 16 * e + 16], pkT[:, e * P:(e + 1) * P],
                                            flat[:, 16 * (e % NB):16 * (e % NB) + 16], start=False, stop=True, skip_group_check=True)
                    ins.then_inc(p_s, 1)

                def both(out_, w_, s, a, b_, start):
                    t_.matmul(out_, w_[:, :], lh[s % 2][:, a:b_], start=start, stop=False, skip_group_check=True)
                    return t_.matmul(out_, w_[:, :], ll[s % 2][:, a:b_], start=False, stop=True, skip_group_check=True)

                def within(s):
                    o, w, dg, first, last = step_shape(s)
                    pe.wait_ge(d_llo, att.at(s + 1))
                    if first and s:
                        pe.wait_ge(d_sub, att.at(s))
                    if s < SAMPLE:
                        both(pb_[:, o:o + w], tri, s, 0, w, first).then_inc(p_tri, 1)
                    else:
                        for j in range(3):
                            c = pb_[:, j * P:(j + 1) * P]
                            ins = both(c, tri, s, j * P, (j + 1) * P, j == 0)
                            for i in range(j):
                                ins = both(c, full, s, i * P, (i + 1) * P, False)
                        ins.then_inc(p_tri, 1)

                def rest(s):
                    o, w, dg, first, last = step_shape(s)
                    pe.wait_ge(d_sub, att.at(s + 1))
                    both(pb_[:, o:o + w], comp, s, 0, w, False).then_inc(p_comp, 1)

                def values(s):
                    o, w, dg, first, last = step_shape(s)
                    pe.wait_ge(a_a, att.at(s + 1))
                    if first:
                        obank[0] = misc()
                    b = obank[0]
                    if s < SAMPLE:
                        kb = STEPS[s][2]
                        ins = t_.matmul(b[:, o:o + w], vn[:, kb, :], aa[s % 2][:, 0:w], start=first, stop=last, skip_group_check=True)
                    else:
                        pe.wait_ge(pv_in, pvn.step(256))
                        t_.matmul(b[:, 0:P], vn[0:NS, BLK, :], aa[s % 2][0:NS, 0:P], start=True, stop=False, skip_group_check=True)
                        for e in range(PAGES * NB):
                            c = 16 * (e % NB)
                            ins = t_.matmul(b[:, c:c + 16], pv[:, e, :], aa[s % 2][:, P + 16 * e:P + 16 * e + 16],
                                            start=False, stop=(e == PAGES * NB - 1), skip_group_check=True)
                    ins.then_inc(p_av, 1)

                def piece(i, k):
                    gr, s = i % 3, (job.base - (0 if i % 3 == 0 and k == 0 else 1)) % 2
                    if k == 0:
                        if gr == 0:
                            begin_job()
                        fbank[0] = free_bank()[:, 0:GROUPS[gr][1]]
                    (h, l), xhi, xlo, b = tall(s, k), part(xh[:, k, :], gr), part(xl[:, k, :], gr), fbank[0]
                    t_.matmul(b, h, xhi, start=(k == 0), stop=False, skip_group_check=True)
                    t_.matmul(b, h, xlo, start=False, stop=False, skip_group_check=True)
                    ins = t_.matmul(b, l, xhi, start=False, stop=(k == KD - 1), skip_group_check=True)
                    if k == KD - 1:
                        ins.then_inc(p_unit, 1)

                fbank = [None]
                for n in range(SLOTS):
                    if n < NSTEP:
                        scores(n)
                    if n >= 3:
                        values(n - 3)
                    for q in range(PIECES * n, PIECES * (n + 1)):
                        if q == PIECES * n + AHEAD and 0 <= n - 2 < NSTEP:
                            within(n - 2)
                        piece(*divmod(q, KD))
                    if n < NG - 1:
                        new_rows(vT, 6, n + 1)
                    if n - 2 in COMPS:
                        rest(n - 2)
                att.step(NSTEP)
                cmp.step(len(COMPS))
                pe.wait_ge(d_so, son.step())
                turned(misc()[0:2, 0:P], so[:, 0:2]).then_inc(p_m, 1)
                turned(misc()[0:2 * NB, 0:P], so[:, 2:18]).then_inc(p_m, 1)

            with loop(pe, NC4, {job: NIN, unit: 3 * NIN, mis: M_ITER, att: NSTEP, cmp: len(COMPS), cwn: 32,
                                pkn[0]: 128, pkn[1]: 128, pvn: 256, son: 1, qn: 1}):
                pair()

            def branches(s, first=False):
                begin_job()
                for i, (hi, lo) in enumerate(((ch, cl), (oh, ol))):
                    if not first:
                        for gr in range(NG):
                            tile(gr, s, hi, lo, range(NC4 * i, NC4 * (i + 1)), NC4 * i)
                        continue
                    bs = [free_bank()[:, 0:GROUPS[gr][1]] for gr in range(NG)]
                    for k in range(NC4):
                        h, l = tall(s, NC4 * i + k)
                        pe.wait_ge(d_xlo, NC4 * i + k + 1)
                        for gr, b in enumerate(bs):
                            xhi, xlo = part(hi[:, k, :], gr), part(lo[:, k, :], gr)
                            t_.matmul(b, h, xhi, start=(k == 0), stop=False, skip_group_check=True)
                            t_.matmul(b, h, xlo, start=False, stop=False, skip_group_check=True)
                            ins = t_.matmul(b, l, xhi, start=False, stop=(k == NC4 - 1), skip_group_check=True)
                            if k == NC4 - 1:
                                ins.then_inc(p_unit, 1)

            branches(0, True)
            branches(1)
            with loop(pe, 3, {job: 2, unit: 12}):
                for s in range(2):
                    branches(s)
            begin_job()
            for gr in range(NG):
                b = free_bank()[:, 0:GROUPS[gr][1]]
                for k in range(KD):
                    pe.wait_ge(d_mrg, NG * k + gr + 1)
                    (h, l), xhi, xlo = tall(0, k), part(bh[:, k, :], gr), part(bl[:, k, :], gr)
                    t_.matmul(b, h, xhi, start=(k == 0), stop=False)
                    t_.matmul(b, h, xlo, start=False, stop=False)
                    ins = t_.matmul(b, l, xhi, start=False, stop=(k == KD - 1))
                ins.then_inc(p_unit, 1)
            begin_job()
            for gr in range(NG):
                tile(gr, 1, bh, bl)
            with loop(pe, 3, {job: 2, unit: 6}):
                for s in range(2):
                    begin_job()
                    for gr in range(NG):
                        tile(gr, s, bh, bl)
            ssn.step(24)
            stat()
            sqn.base = 2 * KD * NG
            pe.wait_ge(x2_in, 32)
            for i in range(NG * KD + 2):
                if i < NG * KD:
                    x_turned(i // KD, i % KD, xn2, xn2s)
                if i >= 2:
                    summed(i - 2)

            xlo = Count()
            xlo.base = 2 * NC4

            def down(s, half, m0=0):
                if not m0:
                    begin_job()
                for m in range(m0, 4):
                    for gr in range(NG):
                        products(gr, [(wh[s][:, k * 512 + m * P:k * 512 + (m + 1) * P], wl[s][:, k * 512 + m * P:k * 512 + (m + 1) * P],
                                       part(fh[:, k, :], gr), part(fl[:, k, :], gr)) for k in range(2)])

            def rows_turned():
                b = misc()
                pe.wait_ge(cwr_in, cwn.step(96))
                pe.sem_inc(pe_held, 1)
                for h in range(2):
                    ins = turned(b[:, h * 20:h * 20 + 20], fr[:, h, :], 20)
                ins.then_inc(p_m, 1)

            def states_turned():
                pe.wait_ge(d_so, son.step())
                b = misc()
                for h in range(2):
                    ins = turned(b[0:18, h * P:(h + 1) * P], fso[:, h, :])
                ins.then_inc(p_m, 1)

            def up(states, first=False):
                rows_turned()
                for h in range(2):
                    if h and states:
                        states_turned()
                    begin_job()
                    for gr in range(NG):
                        if first:
                            pe.wait_ge(g_lo, KD * (gr + 1))
                        tile(gr, (job.base - 1) % 2, bh, bl)

            def ffn(first):
                up(not first, first)
                if not first:
                    pe.wait_ge(d_xlo, xlo.at())
                    down(0, 0)
                    down(1, 1)
                up(True)
                xlo.step(2)

            ffn(True)
            with loop(pe, 10, {job: 6, unit: 36, mis: 4, cwn: 192, son: 2, xlo: 2}):
                ffn(False)
            states_turned()
            pe.wait_ge(d_xlo, xlo.at(-1))
            begin_job()
            six = [(m, gr, free_bank()[:, 0:GROUPS[gr][1]]) for m in range(2) for gr in range(NG)]
            for k in range(2):
                pe.wait_ge(d_xlo, xlo.at(k - 1))
                for m, gr, b in six:
                    h, l = (w[0][:, k * 512 + m * P:k * 512 + (m + 1) * P] for w in (wh, wl))
                    xhi, xlo_ = part(fh[:, k, :], gr), part(fl[:, k, :], gr)
                    t_.matmul(b, h, xhi, start=(k == 0), stop=False, skip_group_check=True)
                    t_.matmul(b, h, xlo_, start=False, stop=False, skip_group_check=True)
                    ins = t_.matmul(b, l, xhi, start=False, stop=(k == 1), skip_group_check=True)
                    if k == 1:
                        ins.then_inc(p_unit, 1)
            down(0, 0, 2)
            down(1, 1)
            pe.wait_ge(p_in, 32)
            for gr in range(NG):
                for k in range(2):
                    x_turned(gr, k, pn, pn[0:NS, BLK, :])
            pe.wait_ge(d_unit, unit.at())
            ssn.step(24)
            sqn.base += KD * NG
            for half in range(2):
                begin_job()
                if half:
                    stat()
                for m in range(4):
                    for gr in range(NG):
                        products(gr, [(wh[half][:, k * 512 + m * P:k * 512 + (m + 1) * P], wl[half][:, k * 512 + m * P:k * 512 + (m + 1) * P],
                                       part(ph[:, k, :], gr), part(pl[:, k, :], gr)) for k in range(2)])
                        if half and NG * m + gr >= 2:
                            summed(NG * m + gr - 2)
            for i in range(NG * KD // 2 - 2, NG * KD):
                summed(i)
            pe.wait_ge(g_lo, 2 * KD * NG)
            with loop(pe, 4, {job: 2, unit: 6}):
                for s in range(2):
                    begin_job()
                    for gr in range(NG):
                        tile(gr, s, bh, bl)
            ssn.step(24)
            stat()
            dx = 2 * KD * NG
            for gr in range(NG):
                for k in range(KD):
                    i = gr * KD + k
                    if i >= 3:
                        pe.wait_ge(a_nat, i - 2)
                        b = ub[unit.base % 3]
                        unit.step()
                    else:
                        b = free_bank()
                    pe.wait_ge(d_x, dx + i + 1)
                    for j, bl_ in enumerate(group_blocks(gr)):
                        w = block_rows(bl_)
                        ins = turned(b[0:w, j * P:(j + 1) * P], y[:, k, bl_ * P:bl_ * P + w])
                    ins.then_inc(p_unit, 1)
            assert job.base == NJOBS, job.base


PAIR_SELF = 13
FFN_SELF = 10

_INS = ["x_prompt", "x_sample", "cache_k", "cache_v", "state_conv", "state_ffn_conv", "page_table", "p_prompt",
        "p_sample", "g_pre_mix", "w_in", "w_conv_a", "w_a", "w_b", "sb_bias", "w_o", "g_post_mix", "g_pre_ffn",
        "w_up", "w_conv_f", "b_conv_f", "w_down", "g_post_ffn", "w_ple", "g_ple_gate", "w_ple_gate", "g_post_ple"]
_OUTS = [("y_prompt", (1, SEQ, D)), ("y_sample", (NB, NT, D)),
         ("k_prompt", (1, 1, SEQ, 8, 64)), ("v_prompt", (1, 1, SEQ, 8, 64)),
         ("conv_prompt", (1, 1, 2, CW)), ("ffn_conv_prompt", (1, 1, 2, 2 * FF)),
         ("k_sample", (1, NB, NT, 8, 64)), ("v_sample", (1, NB, NT, 8, 64)),
         ("conv_sample", (1, NB, 2, CW)), ("ffn_conv_sample", (1, NB, 2, 2 * FF))]


def kernel(**inputs):
    import numpy as np
    import concourse.bacc as bacc
    from concourse.bass_utils import run_bass_kernel_spmd

    nc = bacc.Bacc("TRN2", target_bir_lowering=False, num_devices=1)
    arrays, inp, out = {}, {}, {}
    for name in _INS:
        arrays[f"in_{name}"] = np.ascontiguousarray(inputs[name])
        inp[name] = nc.dram_tensor(f"in_{name}", arrays[f"in_{name}"].shape, mybir.dt.from_np(arrays[f"in_{name}"].dtype),
                                   kind="ExternalInput").ap()
    for name, shape in _OUTS:
        out[name] = nc.dram_tensor(f"out_{name}", shape, F32, kind="ExternalOutput").ap()
    gate_spill = nc.dram_tensor("gate_spill", (2 * KD, P, TOK), F32).ap()
    build(nc, inp, out, gate_spill)
    got = run_bass_kernel_spmd(nc, [arrays], core_ids=[0]).results[0]
    return tuple(got[f"out_{name}"] for name, _ in _OUTS)
```
